# Optimizing a Trainium2 kernel written in Bass

```python
import math
import jax, jax.numpy as jnp
from jax import lax
import numpy as np

D_MODEL = 1024
BATCH = 1
SEQ = 512
DEPTH = 1
DEC_BATCH = 8
DEC_SEQ = 8
PAST_LEN = 1024
PAGE_SIZE = 128

N_META = 16
HA = 4
DQK = 64
DVA = 128
HB = 4
DKB = 128
DVB = 128
CONV_W = 4
CHUNK = 64
QA_W = HA * 2 * DQK
KA_W = HA * 2 * DQK
VA_W = HA * DVA
CONV_DIM = HB * DKB * 2 + HB * DVB
Z_W = HB * DVB
PROJ_W = QA_W + KA_W + VA_W + CONV_DIM + Z_W + 2 * HB
MIX_W = HA * DVA + HB * DVB
HP = 8
NK = 128
N_EXPERTS = NK * NK
DPK = 256
PEER_TOPK = 16
PEER_BLOCK = 128
Q_BLOCK = 128
EPS = 1e-6

kernel_name = 'hymba_diffattn_gdn_peer_step'

def rmsnorm(x, g):
    xf = x.astype(jnp.float32)
    y = xf * lax.rsqrt(jnp.mean(xf * xf, axis=-1, keepdims=True) + EPS)
    return (y * g.astype(jnp.float32)).astype(x.dtype)

def l2norm(x):
    xf = x.astype(jnp.float32)
    return xf * lax.rsqrt(jnp.sum(xf * xf, axis=-1, keepdims=True) + EPS)

def project(xn, w_in, q_norm, k_norm):
    p = xn @ w_in
    cuts = np.cumsum([QA_W, KA_W, VA_W, CONV_DIM, Z_W, HB]).tolist()
    qa, ka, va, qkv_b, z, b_raw, a_raw = jnp.split(p, cuts, axis=-1)
    lead = xn.shape[:-1]
    q = rmsnorm(qa.reshape(lead + (HA, 2, DQK)), q_norm)
    k = rmsnorm(ka.reshape(lead + (HA, 2, DQK)), k_norm)
    v = va.reshape(lead + (HA, DVA))
    return q, k, v, qkv_b, z, b_raw, a_raw

def diff_attn_core(q, k, v, qpos, kpos, kvalid, lam, slopes):
    s = jnp.einsum('bqhcd,bkhcd->bhcqk', q.astype(jnp.float32), k.astype(jnp.float32)) * (DQK ** -0.5)
    dist = jnp.abs(qpos[:, None] - kpos[None, :]).astype(jnp.float32)
    s = s - slopes[:, None, None, None] * dist
    mask = (kpos[None, :] <= qpos[:, None]) & kvalid[None, :]
    p = jax.nn.softmax(jnp.where(mask, s, -jnp.inf), axis=-1)
    w = p[:, :, 0] - lam * p[:, :, 1]
    return jnp.einsum('bhqk,bkhd->bqhd', w, v.astype(jnp.float32))

def diff_attn_prompt(q, k, v, lam, slopes):
    b, t = q.shape[:2]
    nb = -(-t // Q_BLOCK)
    tp = nb * Q_BLOCK
    qp = jnp.pad(q, ((0, 0), (0, tp - t), (0, 0), (0, 0), (0, 0)))
    kp = jnp.pad(k, ((0, 0), (0, tp - t), (0, 0), (0, 0), (0, 0)))
    vp = jnp.pad(v, ((0, 0), (0, tp - t), (0, 0), (0, 0)))
    kpos = jnp.arange(tp)
    kvalid = kpos < t
    qblocks = jnp.moveaxis(qp.reshape((b, nb, Q_BLOCK) + q.shape[2:]), 1, 0)

    def one_block(args):
        i, qb = args
        qpos = i * Q_BLOCK + jnp.arange(Q_BLOCK)
        return diff_attn_core(qb, kp, vp, qpos, kpos, kvalid, lam, slopes)

    o = lax.map(one_block, (jnp.arange(nb), qblocks))
    o = jnp.moveaxis(o, 0, 1).reshape(b, tp, HA, DVA)
    return o[:, :t]

def gdn_inputs(qkv_pre, conv_prev, conv_w, b_raw, a_raw, a_log, dt_bias):
    t = qkv_pre.shape[1]
    xpad = jnp.concatenate([conv_prev.astype(qkv_pre.dtype), qkv_pre], axis=1)
    conv = sum(conv_w[j] * xpad[:, j:j + t] for j in range(CONV_W))
    conv = jax.nn.silu(conv)
    qb, kb, vb = jnp.split(conv, [HB * DKB, 2 * HB * DKB], axis=-1)
    lead = qb.shape[:2]
    q = l2norm(qb.reshape(lead + (HB, DKB))) * (DKB ** -0.5)
    k = l2norm(kb.reshape(lead + (HB, DKB)))
    v = vb.reshape(lead + (HB, DVB)).astype(jnp.float32)
    beta = jax.nn.sigmoid(b_raw.astype(jnp.float32))
    g = -jnp.exp(a_log.astype(jnp.float32)) * jax.nn.softplus(a_raw.astype(jnp.float32) + dt_bias.astype(jnp.float32))
    return q, k, v, g, beta, xpad[:, t:]

def gdn_chunk(S, q, k, v, g, beta):
    q, k, v = (jnp.swapaxes(a, 1, 2) for a in (q, k, v))
    g = jnp.swapaxes(g, 1, 2)
    beta = jnp.swapaxes(beta, 1, 2)
    c = q.shape[2]
    G = jnp.cumsum(g, axis=-1)
    ti = jnp.arange(c)
    incl = ti[:, None] >= ti[None, :]
    strict = ti[:, None] > ti[None, :]
    decay = jnp.where(incl, jnp.exp(jnp.where(incl, G[..., :, None] - G[..., None, :], 0.0)), 0.0)
    kk = jnp.einsum('bhtd,bhsd->bhts', k, k)
    A = jnp.where(strict, beta[..., :, None] * decay * kk, 0.0)
    eG = jnp.exp(G)
    rhs = beta[..., None] * (v - eG[..., None] * jnp.einsum('bhtk,bhvk->bhtv', k, S))
    L = A + jnp.eye(c, dtype=A.dtype)
    delta = lax.linalg.triangular_solve(L, rhs, left_side=True, lower=True, unit_diagonal=True)
    qk = jnp.einsum('bhtd,bhsd->bhts', q, k)
    o = eG[..., None] * jnp.einsum('bhtk,bhvk->bhtv', q, S) + jnp.einsum('bhts,bhsv->bhtv', decay * qk, delta)
    Gl = G[..., -1:]
    S_new = jnp.exp(Gl)[..., None] * S + jnp.einsum('bhsv,bhsk->bhvk', delta, jnp.exp(Gl - G)[..., None] * k)
    return S_new, jnp.swapaxes(o, 1, 2)

def gdn_prompt(q, k, v, g, beta):
    b, t = q.shape[:2]
    n_chunks = (t - N_META) // CHUNK
    s0 = jnp.zeros((b, HB, DVB, DKB), jnp.float32)
    s1, o_meta = gdn_chunk(s0, q[:, :N_META], k[:, :N_META], v[:, :N_META], g[:, :N_META], beta[:, :N_META])

    def to_chunks(a):
        a = a[:, N_META:]
        return jnp.moveaxis(a.reshape((b, n_chunks, CHUNK) + a.shape[2:]), 1, 0)

    def step(s, xs):
        return gdn_chunk(s, *xs)

    s_fin, o_rest = lax.scan(step, s1, (to_chunks(q), to_chunks(k), to_chunks(v), to_chunks(g), to_chunks(beta)))
    o_rest = jnp.moveaxis(o_rest, 0, 1).reshape(b, n_chunks * CHUNK, HB, DVB)
    return jnp.concatenate([o_meta, o_rest], axis=1), s_fin

def merge_heads(oa, ob, z, lam_init, attn_subln, gdn_norm, w_out, dtype):
    b, t = oa.shape[:2]
    ya = rmsnorm(oa, attn_subln) * (1.0 - lam_init)
    yb = rmsnorm(ob, gdn_norm) * jax.nn.silu(z.reshape(b, t, HB, DVB).astype(jnp.float32))
    y = jnp.concatenate([ya.reshape(b, t, HA * DVA), yb.reshape(b, t, HB * DVB)], axis=-1).astype(dtype)
    return y @ w_out

def peer_ffn(xn, wq, keys, u, v):
    lead = xn.shape[:-1]
    xf = xn.reshape(-1, D_MODEL)
    n = xf.shape[0]
    nb = -(-n // PEER_BLOCK)
    xf = jnp.pad(xf, ((0, nb * PEER_BLOCK - n), (0, 0))).reshape(nb, PEER_BLOCK, D_MODEL)

    def block(xb):
        q = (xb @ wq).reshape(-1, HP, 2, DPK // 2)
        s = jnp.einsum('thcd,hcnd->thcn', q, keys).astype(jnp.float32)
        s1, i1 = lax.top_k(s[:, :, 0], PEER_TOPK)
        s2, i2 = lax.top_k(s[:, :, 1], PEER_TOPK)
        cand = (s1[..., :, None] + s2[..., None, :]).reshape(-1, HP, PEER_TOPK * PEER_TOPK)
        sc, ci = lax.top_k(cand, PEER_TOPK)
        e = jnp.take_along_axis(i1, ci // PEER_TOPK, axis=-1) * NK + jnp.take_along_axis(i2, ci % PEER_TOPK, axis=-1)
        gate = jax.nn.softmax(sc, axis=-1)
        h = jnp.einsum('td,thkd->thk', xb, u[e]).astype(jnp.float32)
        w = (gate * jax.nn.gelu(h, approximate=False)).astype(xb.dtype)
        return jnp.einsum('thk,thkd->td', w, v[e])

    y = lax.map(block, xf).reshape(nb * PEER_BLOCK, D_MODEL)[:n]
    return y.reshape(lead + (D_MODEL,))

def setup_inputs(seed: int = 0) -> dict:
    key = jax.random.key(seed)
    ks = jax.random.split(key, 32)
    f32 = jnp.float32

    def nrm(k, shape, s):
        return jax.random.normal(k, shape, f32) * s

    n_pages = PAST_LEN // PAGE_SIZE
    n_used = DEC_BATCH * n_pages
    n_pool = n_used + (n_used + 3) // 4
    page_table = jax.random.permutation(ks[6], n_pool)[:n_used].reshape(DEC_BATCH, n_pages).astype(jnp.int32)
    a_log = jnp.log(jax.random.uniform(ks[16], (DEPTH, HB), f32, 1.0, 16.0))
    dt = jnp.exp(jax.random.uniform(ks[17], (DEPTH, HB), f32, math.log(1e-3), math.log(1e-1)))
    dt_bias = dt + jnp.log(-jnp.expm1(-dt))
    return {
        'x_prompt': nrm(ks[0], (BATCH, SEQ, D_MODEL), 1.0),
        'x_sample': nrm(ks[1], (DEC_BATCH, DEC_SEQ, D_MODEL), 1.0),
        'cache_k': nrm(ks[2], (DEPTH, n_pool, PAGE_SIZE, HA, 2 * DQK), 1.0),
        'cache_v': nrm(ks[3], (DEPTH, n_pool, PAGE_SIZE, HA, DVA), 1.0),
        'state_ssm': nrm(ks[4], (DEPTH, DEC_BATCH, HB, DVB, DKB), 0.1),
        'state_conv': nrm(ks[5], (DEPTH, DEC_BATCH, CONV_W - 1, CONV_DIM), 1.0),
        'page_table': page_table,
        'meta_tokens': nrm(ks[7], (N_META, D_MODEL), 1.0),
        'norm1': 1.0 + nrm(ks[8], (DEPTH, D_MODEL), 0.05),
        'w_in': nrm(ks[9], (DEPTH, D_MODEL, PROJ_W), D_MODEL ** -0.5),
        'conv_w': nrm(ks[10], (DEPTH, CONV_W, CONV_DIM), CONV_W ** -0.5),
        'q_norm': 1.0 + nrm(ks[11], (DEPTH, DQK), 0.05),
        'k_norm': 1.0 + nrm(ks[12], (DEPTH, DQK), 0.05),
        'lam_q1': nrm(ks[13], (DEPTH, DQK), 0.1),
        'lam_k1': nrm(ks[14], (DEPTH, DQK), 0.1),
        'lam_q2': nrm(ks[15], (DEPTH, DQK), 0.1),
        'lam_k2': nrm(ks[18], (DEPTH, DQK), 0.1),
        'attn_subln': 1.0 + nrm(ks[19], (DEPTH, DVA), 0.05),
        'a_log': a_log,
        'dt_bias': dt_bias,
        'gdn_norm': 1.0 + nrm(ks[20], (DEPTH, DVB), 0.05),
        'w_out': nrm(ks[21], (DEPTH, MIX_W, D_MODEL), MIX_W ** -0.5),
        'norm2': 1.0 + nrm(ks[22], (DEPTH, D_MODEL), 0.05),
        'peer_wq': nrm(ks[23], (DEPTH, D_MODEL, HP * DPK), D_MODEL ** -0.5),
        'peer_keys': nrm(ks[24], (DEPTH, HP, 2, NK, DPK // 2), (DPK // 2) ** -0.5),
        'peer_u': nrm(ks[25], (DEPTH, N_EXPERTS, D_MODEL), D_MODEL ** -0.5),
        'peer_v': nrm(ks[26], (DEPTH, N_EXPERTS, D_MODEL), 0.3),
    }

def reference(x_prompt, x_sample, cache_k, cache_v, state_ssm, state_conv, page_table, meta_tokens,
              norm1, w_in, conv_w, q_norm, k_norm, lam_q1, lam_k1, lam_q2, lam_k2, attn_subln,
              a_log, dt_bias, gdn_norm, w_out, norm2, peer_wq, peer_keys, peer_u, peer_v):
    f32 = jnp.float32
    slopes = jnp.exp2(-(8.0 / HA) * jnp.arange(1, HA + 1, dtype=f32))
    b = x_prompt.shape[0]
    db, ds = x_sample.shape[:2]
    meta = jnp.broadcast_to(meta_tokens.astype(x_prompt.dtype)[None], (b, N_META, D_MODEL))
    hp = jnp.concatenate([meta, x_prompt], axis=1)
    hs = x_sample
    t = hp.shape[1]
    n_past = page_table.shape[1] * PAGE_SIZE
    k_p, v_p, k_s, v_s, ssm_p, ssm_s, conv_p, conv_s = [], [], [], [], [], [], [], []
    for l in range(DEPTH):
        lam_init = 0.8 - 0.6 * math.exp(-0.3 * l)
        lam = (jnp.exp(jnp.sum(lam_q1[l].astype(f32) * lam_k1[l].astype(f32)))
               - jnp.exp(jnp.sum(lam_q2[l].astype(f32) * lam_k2[l].astype(f32))) + lam_init)

        xn = rmsnorm(hp, norm1[l])
        qa, ka, va, qkv_b, z, b_raw, a_raw = project(xn, w_in[l], q_norm[l], k_norm[l])
        oa = diff_attn_prompt(qa, ka, va, lam, slopes)
        conv0 = jnp.zeros((b, CONV_W - 1, CONV_DIM), hp.dtype)
        gq, gk, gv, gg, gbeta, conv_new = gdn_inputs(qkv_b, conv0, conv_w[l], b_raw, a_raw, a_log[l], dt_bias[l])
        ob, s_new = gdn_prompt(gq, gk, gv, gg, gbeta)
        hp = hp + merge_heads(oa, ob, z, lam_init, attn_subln[l], gdn_norm[l], w_out[l], hp.dtype)
        hp = hp + peer_ffn(rmsnorm(hp, norm2[l]), peer_wq[l], peer_keys[l], peer_u[l], peer_v[l])
        k_p.append(ka.reshape(b, t, HA, 2 * DQK))
        v_p.append(va)
        ssm_p.append(s_new)
        conv_p.append(conv_new)

        xn = rmsnorm(hs, norm1[l])
        qa, ka, va, qkv_b, z, b_raw, a_raw = project(xn, w_in[l], q_norm[l], k_norm[l])
        kpast = cache_k[l][page_table].reshape(db, n_past, HA, 2, DQK)
        vpast = cache_v[l][page_table].reshape(db, n_past, HA, DVA)
        k_all = jnp.concatenate([kpast.astype(ka.dtype), ka], axis=1)
        v_all = jnp.concatenate([vpast.astype(va.dtype), va], axis=1)
        qpos = n_past + jnp.arange(ds)
        kpos = jnp.arange(n_past + ds)
        oa = diff_attn_core(qa, k_all, v_all, qpos, kpos, jnp.ones((n_past + ds,), bool), lam, slopes)
        gq, gk, gv, gg, gbeta, conv_new = gdn_inputs(qkv_b, state_conv[l], conv_w[l], b_raw, a_raw, a_log[l], dt_bias[l])
        s_new, ob = gdn_chunk(state_ssm[l].astype(f32), gq, gk, gv, gg, gbeta)
        hs = hs + merge_heads(oa, ob, z, lam_init, attn_subln[l], gdn_norm[l], w_out[l], hs.dtype)
        hs = hs + peer_ffn(rmsnorm(hs, norm2[l]), peer_wq[l], peer_keys[l], peer_u[l], peer_v[l])
        k_s.append(ka.reshape(db, ds, HA, 2 * DQK))
        v_s.append(va)
        ssm_s.append(s_new)
        conv_s.append(conv_new)

    y_prompt = hp[:, N_META:]
    y_sample = hs
    return (y_prompt, y_sample, jnp.stack(k_p), jnp.stack(v_p), jnp.stack(k_s), jnp.stack(v_s),
            jnp.stack(ssm_p), jnp.stack(ssm_s), jnp.stack(conv_p), jnp.stack(conv_s))


_drawn_inputs = setup_inputs


def setup_inputs(seed=0):
    import zlib

    import numpy as np

    out = dict(_drawn_inputs(seed))
    spreads = {}
    factors = {'lam_q2': 4.916}
    for name, (base, spread) in spreads.items():
        noise = np.random.default_rng([zlib.crc32(name.encode()), seed]).standard_normal(out[name].shape)
        drawn = base * np.exp(spread * noise) if base else spread * noise
        out[name] = __import__('jax').numpy.asarray(drawn.astype(out[name].dtype))
    for name, factor in factors.items():
        out[name] = (out[name] * factor).astype(out[name].dtype)
    return out
```

```python
from contextlib import ExitStack

import numpy as np
import concourse.bass as bass
from concourse import mybir
from concourse.alu_op_type import AluOpType as ALU

F32 = mybir.dt.float32
I32 = mybir.dt.int32
U32 = mybir.dt.uint32
ACT = mybir.ActivationFunctionType
AX = mybir.AxisListType

D = 1024
KC = D // 128
SEQ, META = 512, 16
NPOS = META + SEQ
DB, DS = 8, 8
NSAMP = DB * DS
PAST, PAGE = 1024, 128
NPG = PAST // PAGE
NH = 4
DQ = 64
HD = 128
HW = NH * HD
CONV_W = 4
CONV = 3 * HW
CHUNK = 64
PT = SEQ // 128
NT = PT + 1
MROW = NSAMP
LAST = NSAMP + META
TOK = PT * 128 + LAST
ROWS = [128] * PT + [LAST]
OUT_ROWS = [128] * PT + [NSAMP]
OUT_TOK = sum(OUT_ROWS)
EPS = 1e-6
NEG = -1.0e30
HP, NK, TOPK = 8, 128, 16
SLOTS = HP * TOPK
NEXP = NK * NK
SETS = 2 * HP
LAM_INIT = 0.8 - 0.6
SLOPES = [2.0 ** (-(8.0 / NH) * (h + 1)) for h in range(NH)]

QC, KCOL, VC, CC, ZC, BC = 0, HW, 2 * HW, 3 * HW, 3 * HW + CONV, 4 * HW + CONV
SECTIONS = [("ba", BC, 2 * NH), ("conv", CC, HW), ("conv", CC + HW, HW), ("conv", CC + 2 * HW, HW),
            ("k", KCOL, HW), ("q", QC, HW), ("v", VC, HW), ("z", ZC, HW)]
NSEC = len(SECTIONS)
NCONVU = 3 * NT

PRE_PROMPT = CONV_W - 1
PRE_SAMPLE = PRE_PROMPT + NPOS
PRE_STEP = DS + CONV_W - 1
PRE_ROWS = PRE_SAMPLE + DB * PRE_STEP

LEVELS = 6
LAST_LEVELS = 4
GDN_TILES = [PT] + list(range(PT))


def constants():
    p = np.arange(128)[:, None]
    t = np.arange(128)[None, :]
    out = {"ident": (p == t).astype(np.float32), "ones": np.ones((128, 128), np.float32)}
    u = np.arange(META + SEQ)[None, :]
    dist = META + p - (u - (SEQ - 128))
    nb = np.where(dist >= 0, -dist, NEG).astype(np.float32)
    out["bias_prompt"] = np.concatenate([nb * s for s in SLOPES], axis=1)
    r = np.arange(128)
    slope = np.array(SLOPES)[(r // 16) % NH][:, None]
    tok = (r % DS)[:, None]
    out["bias_past"] = (-slope * np.abs(PAST + tok - np.arange(PAST)[None, :])).astype(np.float32)
    new = []
    for pair in range(DB // 2):
        seq = 2 * pair + (r // 64)[:, None]
        key = np.arange(NSAMP)[None, :]
        d = tok - key % DS
        new.append(np.where((key // DS == seq) & (d >= 0), -slope * d, NEG).astype(np.float32))
    out["bias_new"] = np.concatenate(new, axis=1)
    col = np.arange(64)[None, :]
    rr = r[:, None]
    out["fold"] = ((col // 32 == rr // 64) & ((col // 8) % NH == (rr // 16) % NH)
                   & (col % 8 == rr % 8)).astype(np.float32)
    out["first"] = ((rr // 8) % 2 == 0).astype(np.float32)
    out["second"] = ((rr // 8) % 2 == 1).astype(np.float32)
    group_p = p // CHUNK
    group_l = np.where(p < NSAMP, p // DS, np.where(p < LAST, 100, 200 + p))
    for name, g in (("prompt", group_p), ("last", group_l)):
        same = g == g.T
        out[f"upto_{name}"] = (same & (p <= t)).astype(np.float32)
        out[f"after_{name}"] = (same & (p > t)).astype(np.float32)
        for lv in range(LEVELS):
            size = 1 << lv
            m = same & (p // (2 * size) == t // (2 * size)) & (p % (2 * size) < size) & (t % (2 * size) >= size)
            if name == "last" and lv >= LAST_LEVELS:
                continue
            out[f"level{lv}_{name}"] = m.astype(np.float32)
    out["chunk_rows"] = np.concatenate([np.repeat((group_p == c).astype(np.float32), 128, 1) for c in range(2)], 1)
    out["meta_rows"] = np.repeat(((p >= MROW) & (p < LAST)).astype(np.float32), 128, 1)
    out["seq_rows"] = ((p < NSAMP) & (p // DS == np.arange(DB)[None, :])).astype(np.float32)
    out["iota"] = np.tile(np.arange(TOPK, dtype=np.float32)[None, :], (128, 1))
    return out


CONSTS = constants()
CONST_AT = {}
_at = 0
for _n, _a in CONSTS.items():
    CONST_AT[_n] = (_at, _a.shape[1])
    _at += _a.shape[1]
NCONST = _at


class Count:

    def __init__(self, eng):
        self.eng, self.n = eng, {}

    def inc(self, ins, sem):
        ins.then_inc(sem, 1)
        self.n[sem.name] = self.n.get(sem.name, 0) + 1
        return self.n[sem.name]

    def done(self, ins, sem):
        self.eng.wait_ge(sem, self.inc(ins, sem))


def hybrid_step(nc: bass.Bass, i, o, const):
    ctx = ExitStack()
    with ctx:
        def keep(name, shape, dt=F32):
            return ctx.enter_context(nc.sbuf_tensor("sb_" + name, shape, dt))

        sems = []

        def sem(name):
            sems.append(nc.alloc_semaphore(name))
            return sems[-1]

        consts = keep("consts", [128, NCONST])

        def c(name, rows=128, width=None, p0=0):
            at, w = CONST_AT[name]
            return consts[p0:p0 + rows, at:at + (width or w)]

        mix = keep("mix", [128, NT, D])
        minus_half = keep("minus_half", [128, 16])
        front = ExitStack()

        def front_buffer(name, shape, dt=F32):
            return front.enter_context(nc.sbuf_tensor("sb_" + name, shape, dt))

        qT = front_buffer("qT", [128, NH, TOK])
        kT = front_buffer("kT", [128, NH, TOK])
        vtok = front_buffer("vtok", [128, NT, HW])
        vmeta = front_buffer("vmeta", [META, HW])
        ztok = front_buffer("ztok", [128, NT, HW])
        ba = front_buffer("ba", [128, NT, 2 * NH])
        bank = [ctx.enter_context(nc.psum_tensor(f"bank{b}", [128, 512], F32)) for b in range(8)]
        pre = nc.dram_tensor("pre_conv", [PRE_ROWS, CONV], F32).ap()

        def stage(names):
            out = {}
            with ExitStack() as s:
                for name, (shape, dt) in names.items():
                    out[name] = s.enter_context(nc.sbuf_tensor("sb_" + name, shape, dt))
            return out

        A = stage({
            "xin": ([128, 2, D], F32), "xn": ([128, 2, D], F32), "xnT": ([128, KC, TOK], F32),
            "w": ([128, 2, KC, HW], F32), "pre_out": ([128, 3, HW], F32), "sq": ([128, D], F32),
            "sq8": ([128, 2, HW], F32), "qkn": ([128, 2, HW], F32), "gain1": ([128, D], F32),
            "gain_q": ([128, DQ], F32), "gain_k": ([128, DQ], F32), "ss": ([128, NT], F32),
            "ms": ([128, NT], F32), "zrow": ([PRE_PROMPT, CONV], F32), "rstd": ([128, NT], F32), "ss8": ([128, 2, 8], F32),
            "ms8": ([128, 2, 8], F32), "rstd8": ([128, 2, 8], F32),
        })
        s_const = sem("constants_loaded")
        s_x = [sem(f"x_loaded{r}") for r in range(2)]
        s_gain = sem("gains_loaded")
        s_half = sem("minus_half_set")
        s_ba0 = sem("ba_cleared")
        s_ss = sem("x_squares_summed")
        s_ms = sem("x_mean_square")
        s_rstd = sem("x_rstd")
        s_xn = sem("x_normed")
        s_xnT_ps = sem("x_transposed")
        s_xnT = sem("xT_copied")
        s_w = [sem(f"w_loaded{r}") for r in range(2)]
        s_proj = sem("projected")
        s_bank = [sem(f"proj_bank_read{b}") for b in range(4)]
        s_pre_cp = sem("pre_copied")
        s_pre_st = [sem(f"pre_stored{r}") for r in range(3)]
        s_hist = sem("conv_history_stored")
        s_zrow = sem("zero_row_set")
        s_sq8 = sem("qk_squared")
        s_ss8 = sem("qk_squares_summed")
        s_ms8 = sem("qk_mean_square")
        s_rstd8 = sem("qk_rstd")
        s_gq = sem("q_gain_scaled")
        s_qkn = sem("qk_normed")
        s_qkT_ps = sem("qk_transposed")
        s_qkT = sem("qkT_copied")
        s_kst = [sem(f"k_stored{r}") for r in range(2)]
        s_vcp = sem("v_copied")
        s_vst = sem("v_stored")
        s_vmeta = sem("v_meta_moved")
        units = [(g, t) for g in range(NSEC) for t in range(NT)]
        QK0 = 4 * NT

        def unit_bank(n):
            return bank[2 + n % 4]

        def token_cols(t, key=False):
            if not key:
                return [(0, ROWS[t], 128 * t)]
            return [(0, 128, META + 128 * t)] if t < PT else [(0, NSAMP, NPOS), (MROW, META, 0)]

        def out_rows(t):
            return [(0, 128, True, META + 128 * t)] if t < PT else [(0, NSAMP, False, 0), (MROW, META, True, 0)]

        def pre_rows(t):
            if t < PT:
                r = PRE_PROMPT + META + 128 * t
                return [(0, 128, pre[r:r + 128, :])]
            samp = pre[PRE_SAMPLE:, :].rearrange("(b r) c -> b r c", r=PRE_STEP)[:, CONV_W - 1:, :]
            return [(0, NSAMP, samp), (MROW, META, pre[PRE_PROMPT:PRE_PROMPT + META, :])]

        V = [128, NH, HD]
        B = stage({
            "cv": ([128, 2, CONV_W, HW], F32), "cw": ([128, CONV_W, CONV], F32), "cs": ([128, CONV], F32),
            "kq": ([128, 2, NH, HD], F32), "kb": (V, F32), "qg": (V, F32), "kbg": (V, F32), "kd": (V, F32), "vb": (V, F32),
            "knT": (V, F32), "kqT": ([128, NH, 2, 128], F32), "wq": ([128, 2, NH, 128], F32),
            "DT": (V, F32), "AT": (V, F32), "PT": (V, F32), "MT": ([128, 2, NH, HD], F32), "X": (V, F32), "XT": (V, F32),
            "Y": (V, F32), "U": (V, F32), "dl": (V, F32), "ST": ([128, 2, NH, HD], F32), "gb": (V, F32),
            "sS": ([128, NH, DB, HD], F32), "sST": ([128, DB, HD], F32), "kdw": ([NSAMP, DB, HD], F32), "oT": ([128, 2, NH, NSAMP], F32),
            "gn": ([128, HD], F32), "dtb": ([128, NH], F32), "nega": ([128, NH], F32), "gw": ([NSAMP, DB, NH], F32),
            "beta": ([128, NT, NH], F32), "g": ([128, NT, NH], F32), "ta": ([128, NT, NH], F32), "tb": ([128, NT, NH], F32),
            "tc": ([128, NT, NH], F32), "Gs": ([128, 8], F32), "eG": ([128, 8], F32), "eT": ([128, 40], F32),
            "bss": ([128, 8], F32), "bms": ([128, 8], F32), "brs": ([128, 8], F32),
            "oss": ([128, NH], F32), "oms": ([128, NH], F32), "ors": ([128, NH], F32),
        })
        s_bg = sem("conv_weights_loaded")
        s_bgp = sem("gdn_vectors_loaded")
        s_gate = sem("gate_steps_dve")
        s_gatea = sem("gate_steps_act")
        s_cv = [sem(f"conv_rows_loaded{r}") for r in range(2)]
        s_cvo = sem("conv_outputs_stored")
        s_conv = sem("conv_steps")
        s_cs = sem("conv_silu")
        s_bsq = sem("gdn_squared")
        s_bss = sem("gdn_squares_summed")
        s_bms = sem("gdn_mean_square")
        s_brs = sem("gdn_rstd")
        s_brq = sem("gdn_q_scaled")
        s_gb = sem("decay_rows_spread")
        s_psG = sem("decay_summed")
        s_eg = sem("decay_exp")
        s_dT = sem("decay_differences")
        s_DT = sem("decay_matrix_exp")
        s_DTm = sem("decay_matrix_masked")
        s_vec = sem("gdn_vectors")
        s_tr = sem("gdn_transposed")
        s_tc = sem("gdn_transposes_copied")
        s_kk = sem("key_products")
        s_at = sem("key_products_decayed")
        s_x0 = sem("inverse_started")
        s_mt = sem("level_masked")
        s_y = sem("level_left_product")
        s_yc = sem("level_left_copied")
        s_xp = sem("level_products")
        s_xx = sem("level_applied")
        s_uw = sem("inverse_applied")
        s_uwc = sem("inverse_applied_copied")
        s_st0 = sem("state_cleared")
        s_pa = sem("state_read_out")
        s_dl = sem("delta_ready")
        s_pst = sem("state_update_product")
        s_po = sem("gdn_out")
        s_st = sem("state_updated")
        s_sS = sem("sample_state_loaded")
        s_sT = sem("sample_state_transposed")
        s_sTc = sem("sample_state_copied")
        s_oT = sem("sample_state_read_out")
        s_oTc = sem("sample_read_out_copied")
        s_kdw = sem("sample_keys_spread")
        s_sn = sem("sample_update_product")
        s_snd = sem("sample_state_steps")
        s_sst = sem("sample_state_stored")
        s_osq = sem("gdn_out_squared")
        s_oss = sem("gdn_out_squares_summed")
        s_oms = sem("gdn_out_mean_square")
        s_ors = sem("gdn_out_rstd")
        s_ob = sem("gdn_out_steps")
        s_fT = sem("final_state_transposed")
        s_fTc = sem("final_state_copied")
        s_fst = sem("final_state_stored")
        LEVEL_BANKS = ((2, 3, 4), (5, 0, 1))
        samp_rows = pre[PRE_SAMPLE:, :].rearrange("(b r) c -> b r c", r=PRE_STEP)

        def levels(t):
            return LAST_LEVELS if t == PT else LEVELS

        def kind(t):
            return "last" if t == PT else "prompt"

        def chunks(t):
            return [(MROW, META, 0)] if t == PT else [(0, CHUNK, 0), (CHUNK, CHUNK, NH)]

        def before(u, per):
            return sum(per(GDN_TILES[m]) for m in range(u))

        def conv_dmas(u):
            return sum(2 * CONV_W if m // 3 == 0 else CONV_W for m in range(u % 2, u + 1, 2))

        KRING = 3
        C = stage({
            "S": ([128, 2, 2, NPOS], F32), "nm": ([128, 2, 2], F32), "Z": ([128, 2, 2], F32), "rz": ([128, 2, 2], F32),
            "wT": ([128, 2, SEQ], F32), "wTm": ([META, 2, 128], F32), "sqa": ([128, HW], F32),
            "ass": ([128, NH], F32), "ams": ([128, NH], F32), "ars": ([128, NH], F32), "ga": ([128, HD], F32),
            "lam4": ([128, 4, DQ], F32), "lam": ([128, 4], F32), "sgn": ([128, 2], F32),
            "pages": ([1, DB * NPG], I32), "kpage": ([128, KRING, HW], F32), "KT": ([128, 2, NH, PAST], F32),
            "V": ([128, 3, NPG, HW], F32), "Qd": ([128, NH, DB, 64], F32), "Sd": ([128, 2, PAST + NSAMP], F32),
            "dm": ([128, 2, 1], F32), "dZ": ([128, 2, 1], F32), "fold": ([128, 64], F32), "wd": ([128, NPG + 1, 64], F32), "oTs": ([128, NH, NSAMP], F32),
        })
        s_cin = sem("attention_vectors_loaded")
        s_lam = sem("lambda_steps")
        s_lame = sem("lambda_exp")
        s_sc = sem("scores")
        s_scm = sem("first_meta_scores")
        s_sadd = sem("scores_biased")
        s_e = sem("scores_exp")
        s_wn = sem("weights_steps")
        s_wt = sem("weights_transposed")
        s_wtc = sem("weights_copied")
        s_pv = sem("values_weighted")
        s_asq = sem("attn_out_squared")
        s_ass = sem("attn_out_squares_summed")
        s_ams = sem("attn_out_mean_square")
        s_ars = sem("attn_out_rstd")
        s_oa = sem("attn_out_steps")
        s_pg = sem("page_table_loaded")
        s_kp = [sem(f"key_page_loaded{r}") for r in range(KRING)]
        s_vp = [sem(f"value_pages_loaded{r}") for r in range(3)]
        s_qd0 = sem("sample_queries_cleared")
        s_qd = sem("sample_queries_spread")
        s_ktp = sem("key_page_transposed")
        s_kta = sem("key_page_copied_act")
        s_ktd = sem("key_page_copied_dve")
        s_ds = sem("sample_scores")
        s_dadd = sem("sample_scores_biased")
        s_de = sem("sample_scores_exp")
        s_dn = sem("sample_weight_steps")
        s_dw = sem("sample_weights")
        s_dwc = sem("sample_weights_copied")
        s_dpv = sem("sample_values_weighted")
        s_doc = sem("sample_out_copied")
        s_dot = sem("sample_out_transposed")
        ATT = [(t, h) for t in range(PT) for h in range(NH)]
        NPAIR = DB // 2

        def query_rows(t):
            return 0, 128, 128 * t, 128 * (t + 1)

        left_B = [(s_po, before(NT, lambda t: len(chunks(t)) + (t == PT))), (s_ob, 3 * NT), (s_fst, 16), (s_sst, 16 * NH), (s_fTc, 1)]

        def pre_count(n):
            return sum(2 if m % NT == PT else 1 for m in range(n % 3, n + 1, 3))

        left_A = ([(s_proj, NT * NSEC), (s_hist, 32), (s_kst[0], 16 * (NT + 3) // 2), (s_kst[1], 16 * (NT // 2)), (s_qkT, 2 * NT)]
                  + [(s_pre_st[r], 16 * pre_count(NCONVU - 3 + r)) for r in range(3)] + [(s_bank[r], len(units) // 4) for r in range(4)])

        stores = [(s_kst[0], 16 * (NT + 3) // 2), (s_kst[1], 16 * (NT // 2)), (s_vst, 16 * (NT + 1)), (s_vmeta, 16),
                  (s_cvo, 32), (s_sst, 16 * NH), (s_fst, 16)]

        with nc.Block() as block:

            @block.sync
            def _(sp):
                count = Count(sp)
                sp.dma_start(consts[:, :], const).then_inc(s_const, 16)
                sections_w = i["w_in"][0].rearrange("(k p) n -> p k n", p=128)

                def load_x(t):
                    if t >= 2:
                        sp.wait_ge(s_xn, t - 1)
                    if t < PT:
                        sp.dma_start(A["xin"][:, t % 2, :], i["x_prompt"][0, 128 * t:128 * t + 128, :]).then_inc(s_x[t % 2], 16)
                    else:
                        sp.dma_start(A["xin"][0:NSAMP, t % 2, :], i["x_sample"].rearrange("b s d -> (b s) d")).then_inc(s_x[t % 2], 16)
                        sp.dma_start(A["xin"][MROW:LAST, t % 2, :], i["meta_tokens"]).then_inc(s_x[t % 2], 16)

                def load_w(g):
                    _, c0, width = SECTIONS[g]
                    if g >= 2:
                        sp.wait_ge(s_proj, NT * (g - 1))
                    sp.dma_start(A["w"][:, g % 2, :, 0:width], sections_w[:, :, c0:c0 + width]).then_inc(s_w[g % 2], 16)

                load_x(0)
                load_x(1)
                load_w(0)
                load_w(1)
                for t in range(2, NT):
                    load_x(t)
                for g in range(2, 6):
                    load_w(g)
                for t in range(NT):
                    sp.wait_ge(s_qkn, t + 1)
                    for r, rows, prompt, first in out_rows(t):
                        dst = (o["k_prompt"][0, 0] if prompt else o["k_sample"][0].rearrange("b s h d -> (b s) h d")).rearrange("r h d -> r (h d)")
                        sp.dma_start(dst[first:first + rows, :], A["qkn"][r:r + rows, t % 2, :]).then_inc(s_kst[t % 2], 16)
                for g in range(6, NSEC):
                    load_w(g)
                sp.wait_ge(s_hist, 32)
                for r in range(3):
                    sp.wait_ge(s_pre_st[r], 16 * pre_count(NCONVU - 3 + r))
                sp.dma_start(o["conv_prompt"][0, 0], pre[PRE_PROMPT + NPOS - 3:PRE_PROMPT + NPOS, :]).then_inc(s_cvo, 16)
                sp.dma_start(o["conv_sample"][0], samp_rows[:, DS:, :]).then_inc(s_cvo, 16)
                for s_last, total in left_A:
                    sp.wait_ge(s_last, total)
                sp.dma_start(B["cw"][:, :, :], i["conv_w"][0:1].broadcast_to([128, CONV_W, CONV])).then_inc(s_bg, 16)
                for h in range(NH):
                    sp.dma_start(B["sS"][:, h, :, :], i["state_ssm"][0, :, h].rearrange("b v k -> v b k")).then_inc(s_sS, 16)
                for m in range(3 * NT):
                    u, sec = divmod(m, 3)
                    t = GDN_TILES[u]
                    if m >= 2:
                        sp.wait_ge(s_cs, m - 1)
                    for j in range(CONV_W):
                        ch = slice(sec * HW, (sec + 1) * HW)
                        if t == PT:
                            sp.dma_start(B["cv"][0:NSAMP, m % 2, j, :], samp_rows[:, j:j + DS, ch]).then_inc(s_cv[m % 2], 16)
                            sp.dma_start(B["cv"][MROW:LAST, m % 2, j, :], pre[j:j + META, ch]).then_inc(s_cv[m % 2], 16)
                        else:
                            r = META + 128 * t + j
                            sp.dma_start(B["cv"][:, m % 2, j, :], pre[r:r + 128, ch]).then_inc(s_cv[m % 2], 16)
                for h in range(NH):
                    sp.wait_ge(s_snd, 3 * (h + 1))
                    sp.dma_start(o["ssm_sample"][0, :, h].rearrange("b v k -> v b k"), B["sS"][:, h, :, :]).then_inc(s_sst, 16)
                sp.wait_ge(s_fTc, 1)
                sp.dma_start(o["ssm_prompt"][0, 0].rearrange("h v k -> v h k"), B["U"][:, :, :]).then_inc(s_fst, 16)
                for s_last, total in left_B:
                    sp.wait_ge(s_last, total)
                sp.dma_start(C["pages"][:, :], i["page_table"].rearrange("b g -> (b g)").rearrange("(a n) -> a n", a=1)).then_inc(s_pg, 16)
                sp.wait_ge(s_pg, 16)
                cached = [i[name].shape[1] - 1 for name in ("cache_k", "cache_v")]
                for b in range(DB + 1):
                    for g in range(NPG if b < DB else 0):
                        n = b * NPG + g
                        page = sp.value_load(C["pages"][0:1, n:n + 1], min_val=0, max_val=cached[0])
                        if n >= KRING:
                            sp.wait_ge(s_ktp, n - KRING + 1)
                        sp.dma_start(C["kpage"][:, n % KRING, :], i["cache_k"][0, bass.ds(page, 1)].rearrange("g p h d -> (g p) (h d)")).then_inc(s_kp[n % KRING], 16)
                    if b == 0:
                        continue
                    v = b - 1
                    if v >= 3:
                        sp.wait_ge(s_dpv, v - 2)
                    for g in range(NPG):
                        n = v * NPG + g
                        page = sp.value_load(C["pages"][0:1, n:n + 1], min_val=0, max_val=cached[1])
                        sp.dma_start(C["V"][:, v % 3, g, :], i["cache_v"][0, bass.ds(page, 1)].rearrange("g p h d -> (g p) (h d)")).then_inc(s_vp[v % 3], 16)
                for s_out, total in stores:
                    sp.wait_ge(s_out, total)

            @block.gpsimd
            def _(pool):
                count = Count(pool)
                pool.dma_start(A["gain1"][:, :], i["norm1"][0:1, :].broadcast_to([128, D])).then_inc(s_gain, 16)
                pool.dma_start(A["gain_q"][:, :], i["q_norm"][0:1, :].broadcast_to([128, DQ])).then_inc(s_gain, 16)
                pool.dma_start(A["gain_k"][:, :], i["k_norm"][0:1, :].broadcast_to([128, DQ])).then_inc(s_gain, 16)
                pool.memset(ba[:, :, :], 0.0).then_inc(s_ba0, 1)
                pool.memset(minus_half[:, :], -0.5).then_inc(s_half, 1)
                pool.memset(A["zrow"][:, :], 0.0).then_inc(s_zrow, 1)
                pool.wait_ge(s_zrow, 1)
                pool.dma_start(pre[0:PRE_PROMPT, :], A["zrow"][:, :]).then_inc(s_hist, 16)
                samp = pre[PRE_SAMPLE:, :].rearrange("(b r) c -> b r c", r=PRE_STEP)
                pool.dma_start(samp[:, 0:CONV_W - 1, :], i["state_conv"][0]).then_inc(s_hist, 16)
                pool.wait_ge(s_half, 1)
                for t in range(NT):
                    rows = ROWS[t]
                    pool.wait_ge(s_ms, t + 1)
                    nc.gpsimd.tensor_tensor(A["rstd"][0:rows, t:t + 1], A["ms"][0:rows, t:t + 1], minus_half[0:rows, 0:1], ALU.pow).then_inc(s_rstd, 1)
                for u in range(2 * NT):
                    rows = ROWS[u % NT]
                    pool.wait_ge(s_ms8, u + 1)
                    nc.gpsimd.tensor_tensor(A["rstd8"][0:rows, u % 2, :], A["ms8"][0:rows, u % 2, :], minus_half[0:rows, 0:8], ALU.pow).then_inc(s_rstd8, 1)
                for s_last, total in left_A:
                    pool.wait_ge(s_last, total)
                for name, src, width in (("gn", "gdn_norm", HD), ("dtb", "dt_bias", NH), ("nega", "a_log", NH)):
                    pool.dma_start(B[name][:, :], i[src][0:1, :].broadcast_to([128, width])).then_inc(s_bgp, 16)
                pool.memset(B["ST"][:, 0, :, :], 0.0).then_inc(s_st0, 1)

                def key_query_rstd(u):
                    rows = ROWS[GDN_TILES[u]]
                    pool.wait_ge(s_bms, u + 1)
                    nc.gpsimd.tensor_tensor(B["brs"][0:rows, :], B["bms"][0:rows, :], minus_half[0:rows, 0:8], ALU.pow).then_inc(s_brs, 1)

                key_query_rstd(0)
                for u, t in enumerate(GDN_TILES):
                    rows = ROWS[t]
                    if u + 1 < len(GDN_TILES):
                        key_query_rstd(u + 1)
                    pool.wait_ge(s_oms, u + 1)
                    nc.gpsimd.tensor_tensor(B["ors"][0:rows, :], B["oms"][0:rows, :], minus_half[0:rows, 0:NH], ALU.pow).then_inc(s_ors, 1)
                for s_last, total in left_B:
                    pool.wait_ge(s_last, total)
                pool.memset(C["Qd"][:, :, :, :], 0.0).then_inc(s_qd0, 1)
                pool.dma_start(C["ga"][:, :], i["attn_subln"][0:1, :].broadcast_to([128, HD])).then_inc(s_cin, 16)
                for n, name in enumerate(("lam_q1", "lam_k1", "lam_q2", "lam_k2")):
                    pool.dma_start(C["lam4"][:, n, :], i[name][0:1, :].broadcast_to([128, DQ])).then_inc(s_cin, 16)
                for t in range(NT):
                    rows = OUT_ROWS[t]
                    pool.wait_ge(s_ams, t + 1)
                    nc.gpsimd.tensor_tensor(C["ars"][0:rows, :], C["ams"][0:rows, :], minus_half[0:rows, 0:NH], ALU.pow).then_inc(s_ars, 1)

            @block.scalar
            def _(act):
                count = Count(act)
                for t in range(NT):
                    rows = ROWS[t]
                    act.wait_ge(s_x[t % 2], 16 * (t // 2 + 1) + 16 * (t == PT))
                    if t:
                        act.wait_ge(s_ss, t)
                    nc.scalar.activation(A["sq"][0:rows, :], A["xin"][0:rows, t % 2, :], ACT.Square,
                                         accum_out=A["ss"][0:rows, t:t + 1]).then_inc(s_ss, 1)
                for t in range(NT):
                    for half in range(2):
                        act.wait_ge(s_xnT_ps, 2 * t + half + 1)
                        nc.scalar.activation(A["xnT"][:, 4 * half:4 * half + 4, 128 * t:128 * t + ROWS[t]],
                                             bank[half][:, 0:4 * ROWS[t]].rearrange("p (k r) -> p k r", k=4), ACT.Copy).then_inc(s_xnT, 1)

                def qk_copy(u):
                    g, t = divmod(u, NT)
                    act.wait_ge(s_qkT_ps, u + 1)
                    src = bank[u % 2][:, 0:NH * ROWS[t]].rearrange("p (h r) -> p h r", h=NH)
                    dst = kT if g == 0 else qT
                    parts = token_cols(t, key=g == 0)
                    for n, (r, rows, c0) in enumerate(parts):
                        ins = nc.scalar.activation(dst[:, :, c0:c0 + rows], src[:, :, r:r + rows], ACT.Copy)
                    ins.then_inc(s_qkT, 1)

                act.wait_ge(s_ba0, 1)
                n_pre = 0
                for n, (g, t) in enumerate(units):
                    name, _, _ = SECTIONS[g]
                    rows = ROWS[t]
                    ps = unit_bank(n)
                    act.wait_ge(s_proj, n + 1)
                    if name == "ba":
                        nc.scalar.activation(ba[0:rows, t, :], ps[0:rows, 0:2 * NH], ACT.Copy).then_inc(s_bank[n % 4], 1)
                    elif name == "conv":
                        r = n_pre % 3
                        if n_pre >= 3:
                            act.wait_ge(s_pre_st[r], 16 * pre_count(n_pre - 3))
                        nc.scalar.activation(A["pre_out"][0:rows, r, :], ps[0:rows, :], ACT.Copy).then_inc(s_bank[n % 4], 1)
                        act.wait_ge(s_bank[n % 4], n // 4 + 1)
                        for row, rr, dram in pre_rows(t):
                            c0 = (g - 1) * HW
                            act.dma_start(dram[..., c0:c0 + HW], A["pre_out"][row:row + rr, r, :]).then_inc(s_pre_st[r], 16)
                        n_pre += 1
                    elif name in ("k", "q"):
                        u = n - QK0
                        if u >= 2:
                            act.wait_ge(s_ss8, u - 1)
                        nc.scalar.activation(A["sq8"][0:rows, u % 2, :], ps[0:rows, :], ACT.Square).then_inc(s_sq8, 1)
                        if u >= 2:
                            qk_copy(u - 2)
                    elif name == "v":
                        if t < 2:
                            qk_copy(2 * NT - 2 + t)
                        nc.scalar.activation(vtok[0:rows, t, :], ps[0:rows, :], ACT.Copy).then_inc(s_bank[n % 4], 1)
                        act.wait_ge(s_bank[n % 4], n // 4 + 1)
                        for row, rr, prompt, first in out_rows(t):
                            dst = (o["v_prompt"][0, 0] if prompt else o["v_sample"][0].rearrange("b s h d -> (b s) h d")).rearrange("r h d -> r (h d)")
                            act.dma_start(dst[first:first + rr, :], vtok[row:row + rr, t, :]).then_inc(s_vst, 16)
                        if t == PT:
                            act.dma_start(vmeta[:, :], vtok[MROW:LAST, t, :]).then_inc(s_vmeta, 16)
                    else:
                        nc.scalar.activation(ztok[0:rows, t, :], ps[0:rows, :], ACT.Silu).then_inc(s_bank[n % 4], 1)
                act.wait_ge(s_gate, 4)
                nc.scalar.activation(B["beta"][:, :, :], ba[:, :, 0:NH], ACT.Exp, scale=-1.0).then_inc(s_gatea, 1)
                nc.scalar.activation(B["nega"][:, :], B["nega"][:, :], ACT.Exp).then_inc(s_gatea, 1)
                nc.scalar.activation(B["tb"][:, :, :], B["tb"][:, :, :], ACT.Exp, scale=-1.0).then_inc(s_gatea, 1)
                act.wait_ge(s_gatea, 3)
                nc.scalar.activation(B["tb"][:, :, :], B["tb"][:, :, :], ACT.Ln, bias=1.0).then_inc(s_gatea, 1)
                st_n = 0
                def silu(u, sec):
                    m, rows = 3 * u + sec, ROWS[GDN_TILES[u]]
                    act.wait_ge(s_conv, 3 * (m + 1))
                    if u and sec == 0:
                        act.wait_ge(s_vec, 7 * u)
                    nc.scalar.activation(B["cs"][0:rows, sec * HW:(sec + 1) * HW], B["cv"][0:rows, m % 2, 0, :], ACT.Silu).then_inc(s_cs, 1)

                def squares(u):
                    rows = ROWS[GDN_TILES[u]]
                    act.wait_ge(s_cs, 3 * u + 2)
                    if u:
                        act.wait_ge(s_tr, 4 * u)
                    nc.scalar.activation(B["kq"][0:rows, :, :, :].rearrange("p a h d -> p (a h d)"), B["cs"][0:rows, 0:2 * HW], ACT.Square).then_inc(s_bsq, 1)

                for sec in range(3):
                    silu(0, sec)
                squares(0)
                for u, t in enumerate(GDN_TILES):
                    rows = ROWS[t]
                    following = u + 1 < len(GDN_TILES)
                    summed = [next(lv for lv in range(levels(t)) if 2 * sec + 2 <= (lv + 1) * 6 // levels(t)) for sec in range(3)]
                    act.wait_ge(s_psG, u + 1)
                    if u:
                        act.wait_ge(s_st, before(u, lambda t: NH * len(chunks(t))))
                    if u == 1:
                        act.wait_ge(s_snd, 3 * NH)
                    nc.scalar.activation(B["Gs"][0:rows, :], bank[0][0:rows, 0:8], ACT.Copy).then_inc(s_eg, 1)
                    nc.scalar.activation(B["eG"][0:rows, :], bank[0][0:rows, 0:8], ACT.Exp).then_inc(s_eg, 1)
                    totals = 40 if t == PT else 8
                    nc.scalar.activation(B["eT"][:, 0:totals], bank[0][:, 8:8 + totals], ACT.Exp).then_inc(s_eg, 1)
                    act.wait_ge(s_dT, NH * (u + 1))
                    nc.scalar.activation(B["DT"][0:rows, :, 0:rows], B["DT"][0:rows, :, 0:rows], ACT.Exp).then_inc(s_DT, 1)
                    if u:
                        act.wait_ge(s_po, before(u, lambda t: len(chunks(t)) + (t == PT)))
                    for n, dst in enumerate((B["knT"], B["kqT"][:, :, 0], B["kqT"][:, :, 1], B["wq"][:, 1])):
                        act.wait_ge(s_tr, 4 * u + n + 1)
                        nc.scalar.activation(dst[:, :, 0:rows], bank[2 + n][:, 0:NH * rows].rearrange("p (h r) -> p h r", h=NH), ACT.Copy).then_inc(s_tc, 1)
                    for lv in range(levels(t)):
                        n = before(u, levels) + lv + 1
                        for pair, (b_y, _, _) in enumerate(LEVEL_BANKS):
                            act.wait_ge(s_y, 2 * (n - 1) + pair + 1)
                            if lv:
                                act.wait_ge(s_xp, 2 * (n - 2) + pair + 1)
                            elif u:
                                act.wait_ge(s_oss, u)
                            nc.scalar.activation(B["Y"][0:rows, 2 * pair:2 * pair + 2, 0:rows], bank[b_y][0:rows, 0:2 * rows].rearrange("p (h r) -> p h r", h=2), ACT.Copy).then_inc(s_yc, 1)
                        if following:
                            for sec in range(3):
                                if summed[sec] + 1 == lv:
                                    silu(u + 1, sec)
                    if following:
                        for sec in range(3):
                            if summed[sec] + 1 == levels(t):
                                silu(u + 1, sec)
                    act.wait_ge(s_uw, u + 1)
                    nc.scalar.activation(B["wq"][:, 0, :, 0:rows], bank[6][:, 0:NH * rows].rearrange("p (h r) -> p h r", h=NH), ACT.Copy).then_inc(s_uwc, 1)
                    nc.scalar.activation(B["U"][0:rows, :, :], bank[5][0:rows, :].rearrange("p (h d) -> p h d", h=NH), ACT.Copy).then_inc(s_uwc, 1)
                    if following:
                        squares(u + 1)
                    if t == PT:
                        for h in range(NH):
                            for half in range(2):
                                act.wait_ge(s_sT, 2 * h + half + 1)
                                if h and half == 0:
                                    act.wait_ge(s_oT, h)
                                nc.scalar.activation(B["sST"][:, 4 * half:4 * half + 4, :].rearrange("p b v -> p (b v)"), bank[2 + half][:, :], ACT.Copy).then_inc(s_sTc, 1)
                        act.wait_ge(s_oT, NH)
                        nc.scalar.activation(B["oT"][:, :, :, :].rearrange("p a h r -> p (a h r)"), bank[4][:, :], ACT.Copy).then_inc(s_oTc, 1)
                    act.wait_ge(s_po, before(u + 1, lambda t: len(chunks(t)) + (t == PT)))
                    act.wait_ge(s_xp, 2 * before(u + 1, levels))
                    nc.scalar.activation(B["Y"][0:rows, :, :].rearrange("p h d -> p (h d)"), bank[0][0:rows, :], ACT.Square).then_inc(s_osq, 1)
                act.wait_ge(s_fT, 1)
                nc.scalar.activation(B["U"][:, :, :].rearrange("p h k -> p (h k)"), bank[2][:, :], ACT.Copy).then_inc(s_fTc, 1)
                act.wait_ge(s_lam, 2)
                nc.scalar.activation(C["lam"][:, 2:4], C["lam"][:, 0:2], ACT.Exp).then_inc(s_lame, 1)

                def att_exp(u):
                    t, h = ATT[u]
                    r0, n, _, nk = query_rows(t)
                    act.wait_ge(s_sadd, 4 * (u + 1))
                    for a in range(2):
                        S = C["S"][r0:r0 + n, u % 2, a, 0:META + nk]
                        nc.scalar.activation(S, S, ACT.Exp, bias=C["nm"][r0:r0 + n, u % 2, a:a + 1], accum_out=C["Z"][r0:r0 + n, u % 2, a:a + 1]).then_inc(s_e, 1)

                def att_copy(u):
                    t, h = ATT[u]
                    r0, n, _, nk = query_rows(t)
                    act.wait_ge(s_wt, u + 1)
                    if u >= 2:
                        act.wait_ge(s_pv, u - 1)
                    nc.scalar.activation(C["wTm"][:, u % 2, 0:n], bank[4 + u % 2][0:META, 128:128 + n], ACT.Copy).then_inc(s_wtc, 1)
                    nc.scalar.activation(C["wT"][:, u % 2, 0:nk], bank[6][:, 0:nk], ACT.Copy).then_inc(s_wtc, 1)

                def att_square(t):
                    rows = OUT_ROWS[t]
                    if t < PT:
                        act.wait_ge(s_pv, NH * (t + 1))
                    if t == PT:
                        act.wait_ge(s_dot, 1)
                    if t:
                        act.wait_ge(s_ass, t)
                    nc.scalar.activation(C["sqa"][0:rows, :], bank[7][0:rows, :], ACT.Square).then_inc(s_asq, 1)

                for u in range(len(ATT) + 1):
                    if u < len(ATT):
                        att_exp(u)
                    if u:
                        att_copy(u - 1)
                        if u % NH == 0:
                            att_square(u // NH - 1)

                def sample_weights_out(p):
                    act.wait_ge(s_dadd, 4 * (p + 1))
                    S = C["Sd"][:, p % 2, :]
                    nc.scalar.activation(S, S, ACT.Exp, bias=C["dm"][:, p % 2, :], accum_out=C["dZ"][:, p % 2, :]).then_inc(s_de, 1)

                def sample_weights_copy(p):
                    act.wait_ge(s_dw, p + 1)
                    if p:
                        act.wait_ge(s_dpv, 2 * p)
                    nc.scalar.activation(C["wd"][:, 0:NPG, :].rearrange("p g r -> p (g r)"), bank[5][:, :], ACT.Copy).then_inc(s_dwc, 1)
                    nc.scalar.activation(C["wd"][0:NSAMP, NPG, :], bank[6][0:NSAMP, 0:64], ACT.Copy).then_inc(s_dwc, 1)

                for p in range(NPAIR):
                    for b in (2 * p, 2 * p + 1):
                        for g in range(0, NPG, 2):
                            n = b * NPG + g
                            if p and n == 2 * p * NPG + 4:
                                sample_weights_out(p - 1)
                            act.wait_ge(s_ktp, n + 1)
                            if b >= 2:
                                act.wait_ge(s_ds, b - 1)
                            nc.scalar.activation(C["KT"][:, b % 2, :, g * PAGE:(g + 1) * PAGE], bank[0][:, :].rearrange("p (h k) -> p h k", h=NH), ACT.Copy).then_inc(s_kta, 1)
                    if p:
                        sample_weights_copy(p - 1)
                sample_weights_out(NPAIR - 1)
                sample_weights_copy(NPAIR - 1)
                act.wait_ge(s_dpv, DB)
                nc.scalar.activation(C["oTs"][:, :, :].rearrange("p h r -> p (h r)"), bank[6][:, 128:128 + NH * NSAMP], ACT.Copy).then_inc(s_doc, 1)
                att_square(PT)

            @block.vector
            def _(dve):
                count = Count(dve)
                dve.wait_ge(s_gain, 48)
                count.done(nc.vector.tensor_scalar(A["gain_q"][:, :], A["gain_q"][:, :], DQ ** -0.5, None, ALU.mult), s_gq)
                for t in range(NT):
                    rows = ROWS[t]
                    dve.wait_ge(s_ss, t + 1)
                    nc.vector.tensor_scalar(A["ms"][0:rows, t:t + 1], A["ss"][0:rows, t:t + 1], 1.0 / D, EPS, ALU.mult, ALU.add).then_inc(s_ms, 1)
                    dve.wait_ge(s_rstd, t + 1)
                    if t >= 2:
                        dve.wait_ge(s_xnT_ps, 2 * (t - 1))
                    nc.vector.scalar_tensor_tensor(A["xn"][0:rows, t % 2, :], A["xin"][0:rows, t % 2, :], A["rstd"][0:rows, t:t + 1],
                                                   A["gain1"][0:rows, :], ALU.mult, ALU.mult).then_inc(s_xn, 1)
                for u in range(2 * NT):
                    g, t = divmod(u, NT)
                    rows, n, r = ROWS[t], QK0 + u, u % 2
                    dve.wait_ge(s_sq8, u + 1)
                    if u >= 2:
                        dve.wait_ge(s_ms8, u - 1)
                    count.done(nc.vector.tensor_reduce(A["ss8"][0:rows, r, :], A["sq8"][0:rows, r, :].rearrange("p (a d) -> p a d", d=DQ), AX.X, ALU.add), s_ss8)
                    nc.vector.tensor_scalar(A["ms8"][0:rows, r, :], A["ss8"][0:rows, r, :], 1.0 / DQ, EPS, ALU.mult, ALU.add).then_inc(s_ms8, 1)
                    dve.wait_ge(s_rstd8, u + 1)
                    if u >= 2:
                        dve.wait_ge(s_qkT_ps, u - 1)
                        if u - 2 < NT:
                            dve.wait_ge(s_kst[r], 16 * (u // 2 + (u - 2 == PT)))
                    qkn = A["qkn"][0:rows, r, :].rearrange("p (a d) -> p a d", d=DQ)
                    nc.vector.tensor_tensor(qkn, unit_bank(n)[0:rows, :].rearrange("p (a d) -> p a d", d=DQ),
                                            A["rstd8"][0:rows, r, :].unsqueeze(2).broadcast_to([rows, 8, DQ]), ALU.mult).then_inc(s_bank[n % 4], 1)
                    dve.wait_ge(s_bank[n % 4], n // 4 + 1)
                    gain = A["gain_k" if g == 0 else "gain_q"]
                    nc.vector.tensor_tensor(qkn, qkn, gain[0:rows, :].unsqueeze(1).broadcast_to([rows, 8, DQ]), ALU.mult).then_inc(s_qkn, 1)
                for s_last, total in left_A:
                    dve.wait_ge(s_last, total)
                dve.wait_ge(s_bg, 16)
                dve.wait_ge(s_bgp, 48)
                a_raw = ba[:, :, NH:2 * NH]
                count.done(nc.vector.tensor_tensor(B["ta"][:, :, :], a_raw, B["dtb"][:, :].unsqueeze(1).broadcast_to([128, NT, NH]), ALU.add), s_gate)
                count.done(nc.vector.tensor_scalar(B["tb"][:, :, :], B["ta"][:, :, :], -1.0, None, ALU.mult), s_gate)
                count.done(nc.vector.tensor_tensor(B["tb"][:, :, :], B["tb"][:, :, :], B["ta"][:, :, :], ALU.max), s_gate)
                count.done(nc.vector.tensor_scalar(B["ta"][:, :, :], B["ta"][:, :, :], 0.0, None, ALU.max), s_gate)
                dve.wait_ge(s_gatea, 4)
                count.done(nc.vector.tensor_tensor(B["ta"][:, :, :], B["ta"][:, :, :], B["tb"][:, :, :], ALU.add), s_gate)
                count.done(nc.vector.tensor_scalar(B["nega"][:, :], B["nega"][:, :], -1.0, None, ALU.mult), s_gate)
                count.done(nc.vector.tensor_tensor(B["g"][:, :, :], B["ta"][:, :, :], B["nega"][:, :].unsqueeze(1).broadcast_to([128, NT, NH]), ALU.mult), s_gate)
                count.done(nc.vector.tensor_scalar(B["tc"][:, :, :], B["beta"][:, :, :], 1.0, None, ALU.add), s_gate)
                count.done(nc.vector.reciprocal(B["beta"][:, :, :], B["tc"][:, :, :]), s_gate)
                dve.wait_ge(s_st0, 1)
                n_chunk = 0

                def per_head(x, rows):
                    return x.unsqueeze(2).broadcast_to([rows, NH, HD])

                def spread_decays(u):
                    t = GDN_TILES[u]
                    rows = ROWS[t]
                    if u:
                        dve.wait_ge(s_psG, u)
                    if t == PT:
                        nc.vector.tensor_tensor(B["gw"][:, :, :], B["g"][0:NSAMP, t, :].unsqueeze(1).broadcast_to([NSAMP, DB, NH]),
                                                c("seq_rows", NSAMP).unsqueeze(2).broadcast_to([NSAMP, DB, NH]), ALU.mult)
                    nc.vector.tensor_copy(B["gb"][0:rows, :, :], per_head(B["g"][0:rows, t, :], rows)).then_inc(s_gb, 1)

                def conv_taps(u, sec):
                    m, rows = 3 * u + sec, ROWS[GDN_TILES[u]]
                    cv = B["cv"][0:rows, m % 2]
                    dve.wait_ge(s_cv[m % 2], 16 * conv_dmas(m))
                    count.done(nc.vector.tensor_tensor(cv, cv, B["cw"][0:rows, :, sec * HW:(sec + 1) * HW], ALU.mult), s_conv)

                def conv_sum(u, sec):
                    m, rows = 3 * u + sec, ROWS[GDN_TILES[u]]
                    cv = B["cv"][0:rows, m % 2]
                    count.done(nc.vector.tensor_tensor(cv[:, 0:2], cv[:, 0:2], cv[:, 2:4], ALU.add), s_conv)
                    count.inc(nc.vector.tensor_tensor(cv[:, 0], cv[:, 0], cv[:, 1], ALU.add), s_conv)

                def square_sums(u):
                    rows = ROWS[GDN_TILES[u]]
                    dve.wait_ge(s_bsq, u + 1)
                    count.done(nc.vector.tensor_reduce(B["bss"][0:rows, :], B["kq"][0:rows, :, :, :].rearrange("p a h d -> p (a h) d"), AX.X, ALU.add), s_bss)
                    nc.vector.tensor_scalar(B["bms"][0:rows, :], B["bss"][0:rows, :], EPS, None, ALU.add).then_inc(s_bms, 1)

                def normed(u):
                    rows = ROWS[GDN_TILES[u]]
                    dve.wait_ge(s_brs, u + 1)
                    count.done(nc.vector.tensor_scalar(B["brs"][0:rows, 0:NH], B["brs"][0:rows, 0:NH], HD ** -0.5, None, ALU.mult), s_brq)
                    dve.wait_ge(s_cs, 3 * (u + 1))
                    if u:
                        dve.wait_ge(s_tr, 4 * u)
                    cs = B["cs"][0:rows, :].rearrange("p (a h d) -> p a h d", a=3, h=NH)
                    nc.vector.tensor_tensor(B["kq"][0:rows, 0], cs[:, 1], per_head(B["brs"][0:rows, NH:2 * NH], rows), ALU.mult).then_inc(s_vec, 1)
                    nc.vector.tensor_tensor(B["kq"][0:rows, 1], cs[:, 0], per_head(B["brs"][0:rows, 0:NH], rows), ALU.mult).then_inc(s_vec, 1)

                spread_decays(0)
                for sec in range(3):
                    conv_taps(0, sec)
                    conv_sum(0, sec)
                square_sums(0)
                normed(0)
                for u, t in enumerate(GDN_TILES):
                    rows = ROWS[t]
                    following = u + 1 < len(GDN_TILES)
                    if u:
                        dve.wait_ge(s_uw, u)
                    cs = B["cs"][0:rows, :].rearrange("p (a h d) -> p a h d", a=3, h=NH)
                    kn, qn = B["kq"][0:rows, 0], B["kq"][0:rows, 1]
                    v = {n: B[n][0:rows] for n in ("kb", "qg", "kbg", "kd", "vb")}
                    beta = per_head(B["beta"][0:rows, t, :], rows)
                    nc.vector.tensor_tensor(v["vb"], cs[:, 2], beta, ALU.mult).then_inc(s_vec, 1)
                    dve.wait_ge(s_vec, 7 * u + 2)
                    nc.vector.tensor_tensor(v["kb"], kn, beta, ALU.mult).then_inc(s_vec, 1)
                    dve.wait_ge(s_eg, 3 * (u + 1))
                    if u:
                        dve.wait_ge(s_at, 4 * u)
                    for h in range(NH):
                        nc.vector.tensor_scalar(B["DT"][0:rows, h, 0:rows], bank[1][0:rows, h * rows:(h + 1) * rows], B["Gs"][0:rows, h:h + 1], 0.0,
                                                ALU.subtract, ALU.min).then_inc(s_dT, 1)
                    dve.wait_ge(s_DT, u + 1)
                    nc.vector.tensor_tensor(B["DT"][0:rows, :, 0:rows], B["DT"][0:rows, :, 0:rows],
                                            c("upto_" + kind(t), rows, rows).unsqueeze(1).broadcast_to([rows, NH, rows]), ALU.mult).then_inc(s_DTm, 1)
                    if u:
                        dve.wait_ge(s_pst, before(u, lambda t: len(chunks(t))))
                    eG = per_head(B["eG"][0:rows, 0:NH], rows)
                    eA = per_head(B["eG"][0:rows, NH:2 * NH], rows)
                    nc.vector.tensor_tensor(v["qg"], qn, eG, ALU.mult).then_inc(s_vec, 1)
                    nc.vector.tensor_tensor(v["kd"], kn, eA, ALU.mult).then_inc(s_vec, 1)
                    dve.wait_ge(s_vec, 7 * u + 4)
                    nc.vector.tensor_tensor(v["kbg"], v["kb"], eG, ALU.mult).then_inc(s_vec, 1)
                    ident = c("ident", rows, rows).unsqueeze(1).broadcast_to([rows, NH, rows])
                    X, XT = B["X"][0:rows, :, 0:rows], B["XT"][0:rows, :, 0:rows]
                    nc.vector.tensor_copy(X, ident).then_inc(s_x0, 1)
                    nc.vector.tensor_copy(XT, ident).then_inc(s_x0, 1)
                    dve.wait_ge(s_kk, u + 1)
                    dve.wait_ge(s_DTm, u + 1)
                    if u:
                        dve.wait_ge(s_po, before(u, lambda t: len(chunks(t)) + (t == PT)))
                    for half in range(2):
                        ps = bank[6 + half][0:rows, :].rearrange("p (h a r) -> p h a r", h=2, a=2)[:, :, :, 0:rows]
                        for a, dst in enumerate((B["AT"], B["PT"])):
                            nc.vector.tensor_tensor(dst[0:rows, 2 * half:2 * half + 2, 0:rows], ps[:, :, a], B["DT"][0:rows, 2 * half:2 * half + 2, 0:rows],
                                                    ALU.mult).then_inc(s_at, 1)
                    dve.wait_ge(s_at, 4 * (u + 1))
                    L0 = before(u, levels)

                    def mask_level(lv):
                        if lv >= 2 or u:
                            dve.wait_ge(s_y, 2 * (L0 + lv - 1))
                        nc.vector.tensor_tensor(B["MT"][0:rows, (L0 + lv) % 2, :, 0:rows], B["AT"][0:rows, :, 0:rows],
                                                c(f"level{lv}_{kind(t)}", rows, rows).unsqueeze(1).broadcast_to([rows, NH, rows]), ALU.mult).then_inc(s_mt, 1)

                    mask_level(0)
                    ahead = [(step, sec) for sec in range(3) for step in (conv_taps, conv_sum)]
                    for lv in range(levels(t)):
                        if lv + 1 < levels(t):
                            mask_level(lv + 1)
                        if following:
                            if lv == 0:
                                spread_decays(u + 1)
                            for step, sec in ahead[lv * len(ahead) // levels(t):(lv + 1) * len(ahead) // levels(t)]:
                                step(u + 1, sec)
                        for pair, (_, b_x, b_xt) in enumerate(LEVEL_BANKS):
                            dve.wait_ge(s_xp, 2 * (L0 + lv) + pair + 1)
                            for x, b in ((X, b_x), (XT, b_xt)):
                                dst = x[:, 2 * pair:2 * pair + 2]
                                nc.vector.tensor_tensor(dst, dst, bank[b][0:rows, 0:2 * rows].rearrange("p (h r) -> p h r", h=2), ALU.subtract).then_inc(s_xx, 1)
                    dve.wait_ge(s_uwc, 2 * (u + 1))
                    if t == PT:
                        dve.wait_ge(s_pa, 1)
                        nc.vector.tensor_tensor(B["dl"][0:NSAMP, :, :], B["U"][0:NSAMP, :, :], bank[7][0:NSAMP, :].rearrange("p (h d) -> p h d", h=NH), ALU.subtract).then_inc(s_dl, 1)
                        for h in range(NH):
                            if h:
                                dve.wait_ge(s_sn, h)
                            nc.vector.tensor_tensor(B["kdw"][:, :, :], B["kd"][0:NSAMP, h, :].unsqueeze(1).broadcast_to([NSAMP, DB, HD]),
                                                    c("seq_rows", NSAMP).unsqueeze(2).broadcast_to([NSAMP, DB, HD]), ALU.mult).then_inc(s_kdw, 1)
                            count.done(nc.vector.tensor_tensor(B["sS"][:, h, :, :], B["sS"][:, h, :, :],
                                                               B["eT"][:, 8:40].rearrange("p (b h) -> p b h", h=NH)[:, :, h].unsqueeze(2).broadcast_to([128, DB, HD]), ALU.mult), s_snd)
                            dve.wait_ge(s_sn, h + 1)
                            for half in range(2):
                                new = B["sS"][:, h, 4 * half:4 * half + 4, :].rearrange("p b k -> p (b k)")
                                count.inc(nc.vector.tensor_tensor(new, new, bank[5 + half][:, :], ALU.add), s_snd)
                    for r0, n, e0 in chunks(t):
                        pa = n_chunk + 2
                        dve.wait_ge(s_pa, pa)
                        nc.vector.tensor_tensor(B["dl"][r0:r0 + n, :, :], B["U"][r0:r0 + n, :, :],
                                                bank[7][r0:r0 + n, :].rearrange("p (h d) -> p h d", h=NH), ALU.subtract).then_inc(s_dl, 1)
                        if following and e0 == 0:
                            square_sums(u + 1)
                        dve.wait_ge(s_pst, n_chunk + 1)
                        for h in range(NH):
                            nc.vector.scalar_tensor_tensor(B["ST"][:, (n_chunk + 1) % 2, h, :], B["ST"][:, n_chunk % 2, h, :], B["eT"][:, e0 + h:e0 + h + 1],
                                                           bank[1][:, h * HD:(h + 1) * HD], ALU.mult, ALU.add).then_inc(s_st, 1)
                        n_chunk += 1
                        dve.wait_ge(s_st, NH * n_chunk)
                    dve.wait_ge(s_osq, u + 1)
                    count.done(nc.vector.tensor_reduce(B["oss"][0:rows, :], B["Y"][0:rows, :, :], AX.X, ALU.add), s_oss)
                    nc.vector.tensor_scalar(B["oms"][0:rows, :], B["oss"][0:rows, :], 1.0 / HD, EPS, ALU.mult, ALU.add).then_inc(s_oms, 1)
                    if following:
                        normed(u + 1)
                    dve.wait_ge(s_ors, u + 1)
                    out = mix[0:rows, t, HW:D].rearrange("p (h d) -> p h d", h=NH)
                    count.done(nc.vector.tensor_tensor(out, bank[0][0:rows, :].rearrange("p (h d) -> p h d", h=NH), per_head(B["ors"][0:rows, :], rows), ALU.mult), s_ob)
                    count.done(nc.vector.tensor_tensor(out, out, B["gn"][0:rows, :].unsqueeze(1).broadcast_to([rows, NH, HD]), ALU.mult), s_ob)
                    count.inc(nc.vector.tensor_tensor(out, out, ztok[0:rows, t, :].rearrange("p (h d) -> p h d", h=NH), ALU.mult), s_ob)
                dve.wait_ge(s_cin, 80)
                for n in range(2):
                    count.inc(nc.vector.tensor_tensor_reduce(out=C["lam4"][:, 2 * n, :], in0=C["lam4"][:, 2 * n, :], in1=C["lam4"][:, 2 * n + 1, :], scale=1.0, scalar=0.0,
                                                             op0=ALU.mult, op1=ALU.add, accum_out=C["lam"][:, n:n + 1]), s_lam)
                dve.wait_ge(s_lame, 1)
                count.done(nc.vector.tensor_tensor(C["lam"][:, 0:1], C["lam"][:, 3:4], C["lam"][:, 2:3], ALU.subtract), s_lam)
                count.done(nc.vector.tensor_scalar(C["lam"][:, 0:1], C["lam"][:, 0:1], -LAM_INIT, None, ALU.add), s_lam)
                minus_lam = C["lam"][:, 0:1]
                count.done(nc.vector.tensor_scalar(C["ga"][:, :], C["ga"][:, :], 1.0 - LAM_INIT, None, ALU.mult), s_lam)
                count.done(nc.vector.tensor_scalar(C["sgn"][:, 0:1], c("second"), minus_lam, None, ALU.mult), s_lam)
                count.done(nc.vector.tensor_tensor(C["sgn"][:, 0:1], C["sgn"][:, 0:1], c("first"), ALU.add), s_lam)

                def att_bias(u):
                    t, h = ATT[u]
                    r0, n, _, nk = query_rows(t)
                    rows = slice(r0, r0 + n)
                    dve.wait_ge(s_sc, u + 1)
                    if u >= 2:
                        dve.wait_ge(s_wt, u - 1)
                    S = C["S"][rows, u % 2]
                    at = CONST_AT["bias_prompt"][0] + h * NPOS + SEQ - 128 - 128 * t
                    meta_bias = consts[rows, at:at + META].unsqueeze(1).broadcast_to([n, 2, META])
                    count.inc(nc.vector.tensor_tensor(S[:, :, 0:META], bank[4 + u % 2][rows, 0:2 * META].rearrange("p (a k) -> p a k", a=2), meta_bias, ALU.add), s_sadd)
                    for a in range(2):
                        count.inc(nc.vector.tensor_tensor(S[:, a, META:META + nk], bank[2 * (u % 2) + a][rows, 0:nk], consts[rows, at + META:at + META + nk], ALU.add), s_sadd)
                    dve.wait_ge(s_sadd, count.n[s_sadd.name])
                    count.inc(nc.vector.tensor_reduce(C["nm"][rows, u % 2, :], S[:, :, 0:META + nk], AX.X, ALU.max, negate=True), s_sadd)

                def att_weights(u):
                    t, h = ATT[u]
                    r0, n, _, nk = query_rows(t)
                    rows = slice(r0, r0 + n)
                    dve.wait_ge(s_e, 2 * (u + 1))
                    S, rz = C["S"][rows, u % 2], C["rz"][rows, u % 2]
                    count.done(nc.vector.reciprocal(rz, C["Z"][rows, u % 2, :]), s_wn)
                    count.done(nc.vector.tensor_tensor(rz[:, 1:2], rz[:, 1:2], minus_lam[rows, :], ALU.mult), s_wn)
                    count.done(nc.vector.tensor_scalar(S[:, 1, 0:META + nk], S[:, 1, 0:META + nk], rz[:, 1:2], None, ALU.mult), s_wn)
                    count.inc(nc.vector.scalar_tensor_tensor(S[:, 0, 0:META + nk], S[:, 0, 0:META + nk], rz[:, 0:1], S[:, 1, 0:META + nk], ALU.mult, ALU.add), s_wn)

                def att_norm(t):
                    rows = OUT_ROWS[t]
                    dve.wait_ge(s_asq, t + 1)
                    count.done(nc.vector.tensor_reduce(C["ass"][0:rows, :], C["sqa"][0:rows, :].rearrange("p (h d) -> p h d", h=NH), AX.X, ALU.add), s_ass)
                    nc.vector.tensor_scalar(C["ams"][0:rows, :], C["ass"][0:rows, :], 1.0 / HD, EPS, ALU.mult, ALU.add).then_inc(s_ams, 1)
                    dve.wait_ge(s_ars, t + 1)
                    out = mix[0:rows, t, 0:HW].rearrange("p (h d) -> p h d", h=NH)
                    count.done(nc.vector.tensor_tensor(out, bank[7][0:rows, :].rearrange("p (h d) -> p h d", h=NH), per_head(C["ars"][0:rows, :], rows), ALU.mult), s_oa)
                    count.inc(nc.vector.tensor_tensor(out, out, C["ga"][0:rows, :].unsqueeze(1).broadcast_to([rows, NH, HD]), ALU.mult), s_oa)

                for u in range(len(ATT) + 1):
                    if u < len(ATT):
                        att_bias(u)
                    if u:
                        att_weights(u - 1)
                        if u > 1 and (u - 1) % NH == 0 and u < len(ATT):
                            att_norm((u - 1) // NH - 1)

                att_norm(PT - 1)
                dve.wait_ge(s_qd0, 1)
                for h in range(NH):
                    for a in range(2):
                        at = (2 * h + a) * DS
                        nc.vector.tensor_copy(C["Qd"][64 * a:64 * a + 64, h, :, at:at + DS],
                                              qT[64 * a:64 * a + 64, h, PT * 128:PT * 128 + NSAMP].rearrange("p (b s) -> p b s", s=DS)).then_inc(s_qd, 1)

                def sample_fold(p):
                    dve.wait_ge(s_de, p + 1)
                    if p:
                        dve.wait_ge(s_dw, p)
                    count.done(nc.vector.reciprocal(C["dZ"][:, p % 2, :], C["dZ"][:, p % 2, :]), s_dn)
                    count.done(nc.vector.tensor_tensor(C["dZ"][:, p % 2, :], C["dZ"][:, p % 2, :], C["sgn"][:, 0:1], ALU.mult), s_dn)
                    count.inc(nc.vector.tensor_scalar(C["fold"][:, :], c("fold"), C["dZ"][:, p % 2, :], None, ALU.mult), s_dn)

                for p in range(NPAIR):
                    for b in (2 * p, 2 * p + 1):
                        for g in range(1, NPG, 2):
                            n = b * NPG + g
                            dve.wait_ge(s_ktp, n + 1)
                            if b >= 2:
                                dve.wait_ge(s_ds, b - 1)
                            nc.vector.tensor_copy(C["KT"][:, b % 2, :, g * PAGE:(g + 1) * PAGE], bank[1][:, :].rearrange("p (h k) -> p h k", h=NH)).then_inc(s_ktd, 1)
                        if p and b % 2 == 0:
                            sample_fold(p - 1)
                    dve.wait_ge(s_ds, 2 * (p + 1))
                    if p >= 2:
                        dve.wait_ge(s_dw, p - 1)
                    S = C["Sd"][:, p % 2, :]
                    for half in range(2):
                        cols = slice(512 * half, 512 * half + 512)
                        count.inc(nc.vector.tensor_tensor(S[:, cols], bank[2 + half][:, :], c("bias_past")[:, cols], ALU.add), s_dadd)
                    count.inc(nc.vector.tensor_tensor(S[:, PAST:], bank[4][:, 0:NSAMP], c("bias_new")[:, NSAMP * p:NSAMP * (p + 1)], ALU.add), s_dadd)
                    dve.wait_ge(s_dadd, 4 * p + 3)
                    count.inc(nc.vector.tensor_reduce(C["dm"][:, p % 2, :], S, AX.X, ALU.max, negate=True), s_dadd)
                sample_fold(NPAIR - 1)
                att_norm(PT)

            @block.tensor
            def _(pe):
                count = Count(pe)
                pe.wait_ge(s_const, 16)
                for t in range(NT):
                    rows = ROWS[t]
                    pe.wait_ge(s_xn, t + 1)
                    for half in range(2):
                        if t:
                            pe.wait_ge(s_xnT, 2 * (t - 1) + half + 1)
                        for k in range(4):
                            kk = 4 * half + k
                            ins = nc.tensor.transpose(bank[half][:, k * rows:(k + 1) * rows], A["xn"][0:rows, t % 2, kk * 128:(kk + 1) * 128],
                                                      c("ident", rows, rows))
                        ins.then_inc(s_xnT_ps, 1)

                def qk_transpose(u):
                    rows = ROWS[u % NT]
                    pe.wait_ge(s_qkn, u + 1)
                    if u >= 2:
                        pe.wait_ge(s_qkT, u - 1)
                    for h in range(NH):
                        ins = nc.tensor.transpose(bank[u % 2][:, h * rows:(h + 1) * rows], A["qkn"][0:rows, u % 2, h * HD:(h + 1) * HD], c("ident", rows, rows))
                    ins.then_inc(s_qkT_ps, 1)

                for n, (g, t) in enumerate(units):
                    name, _, width = SECTIONS[g]
                    rows = ROWS[t]
                    if t == 0:
                        pe.wait_ge(s_w[g % 2], 16 * (g // 2 + 1))
                    if g == 0:
                        pe.wait_ge(s_xnT, 2 * (t + 1))
                    if n >= 4:
                        pe.wait_ge(s_bank[n % 4], n // 4)
                    for k in range(KC):
                        ins = nc.tensor.matmul(unit_bank(n)[0:rows, 0:width], lhsT=A["xnT"][:, k, 128 * t:128 * t + rows],
                                               rhs=A["w"][:, g % 2, k, 0:width], start=k == 0, stop=k == KC - 1)
                    ins.then_inc(s_proj, 1)
                    if QK0 + 2 <= n < QK0 + 2 * NT + 2:
                        qk_transpose(n - 2 - QK0)
                for r in range(4):
                    pe.wait_ge(s_bank[r], len(units) // 4)
                pe.wait_ge(s_qkT, 2 * NT)
                n_chunk = 0
                for u, t in enumerate(GDN_TILES):
                    rows = ROWS[t]
                    L0 = before(u, levels)
                    pe.wait_ge(s_gb, u + 1)
                    if u:
                        pe.wait_ge(s_ob, 3 * u - 2)
                        pe.wait_ge(s_st, NH * n_chunk)
                    g = B["g"][0:rows, t, :]
                    nc.tensor.matmul(bank[0][0:rows, 0:NH], lhsT=c("upto_" + kind(t), rows, rows), rhs=g, start=True, stop=True)
                    nc.tensor.matmul(bank[0][0:rows, NH:2 * NH], lhsT=c("after_" + kind(t), rows, rows), rhs=g, start=True, stop=True)
                    if t == PT:
                        nc.tensor.matmul(bank[0][:, 8:12], lhsT=c("meta_rows", rows, 128), rhs=g, start=True, stop=True)
                        nc.tensor.matmul(bank[0][:, 12:16], lhsT=c("meta_rows", rows, 128), rhs=g, start=True, stop=True)
                        nc.tensor.matmul(bank[0][:, 16:48], lhsT=c("ones", NSAMP, 128), rhs=B["gw"][:, :, :].rearrange("p b h -> p (b h)"), start=True, stop=True)
                    else:
                        for cc in range(2):
                            at = c("chunk_rows")[:, 128 * cc:128 * cc + 128]
                            nc.tensor.matmul(bank[0][:, 8 + NH * cc:8 + NH * cc + NH], lhsT=at, rhs=g, start=True, stop=True)
                    for h in range(NH):
                        ins = nc.tensor.matmul(bank[1][:, h * rows:(h + 1) * rows], lhsT=B["gb"][0:rows, h, :], rhs=c("upto_" + kind(t), rows, rows), start=True, stop=True)
                    ins.then_inc(s_psG, 1)
                    for n, (src, need) in enumerate(((B["kq"][:, 0], 1), (B["kb"], 4), (B["kq"][:, 1], 2), (B["qg"], 5))):
                        pe.wait_ge(s_vec, 7 * u + need)
                        if u and n == 3:
                            pe.wait_ge(s_uwc, 2 * u)
                        if u:
                            pe.wait_ge(s_xx, 4 * L0)
                        for h in range(NH):
                            ins = nc.tensor.transpose(bank[2 + n][:, h * rows:(h + 1) * rows], src[0:rows, h, :], c("ident", rows, rows))
                        ins.then_inc(s_tr, 1)
                    pe.wait_ge(s_tc, 4 * u + 3)
                    if u:
                        pe.wait_ge(s_dl, n_chunk + 1)
                    for h in range(NH):
                        at = (h % 2) * 256
                        ps = bank[6 + h // 2][0:rows, at:at + 256].rearrange("p (a r) -> p a r", a=2)[:, :, 0:rows]
                        ins = nc.tensor.matmul(ps, lhsT=B["knT"][:, h, 0:rows], rhs=B["kqT"][:, h, :, 0:rows], start=True, stop=True)
                    ins.then_inc(s_kk, 1)
                    pe.wait_ge(s_x0, 2 * (u + 1))
                    pe.wait_ge(s_tc, 4 * (u + 1))
                    pe.wait_ge(s_eg, 3 * (u + 1))
                    pe.wait_ge(s_dT, NH * (u + 1))
                    for lv in range(levels(t)):
                        n = L0 + lv
                        pe.wait_ge(s_mt, n + 1)
                        for pair, (b_y, _, _) in enumerate(LEVEL_BANKS):
                            if lv:
                                pe.wait_ge(s_xx, 4 * (n - 1) + 2 * (pair + 1))
                            for k in range(2):
                                h = 2 * pair + k
                                ins = nc.tensor.matmul(bank[b_y][0:rows, k * rows:(k + 1) * rows], lhsT=B["MT"][0:rows, n % 2, h, 0:rows], rhs=B["X"][0:rows, h, 0:rows], start=True, stop=True)
                            ins.then_inc(s_y, 1)
                        for pair, (_, b_x, b_xt) in enumerate(LEVEL_BANKS):
                            pe.wait_ge(s_yc, 2 * n + pair + 1)
                            for k in range(2):
                                h = 2 * pair + k
                                nc.tensor.matmul(bank[b_x][0:rows, k * rows:(k + 1) * rows], lhsT=B["XT"][0:rows, h, 0:rows], rhs=B["Y"][0:rows, h, 0:rows], start=True, stop=True)
                            for k in range(2):
                                h = 2 * pair + k
                                ins = nc.tensor.matmul(bank[b_xt][0:rows, k * rows:(k + 1) * rows], lhsT=B["Y"][0:rows, h, 0:rows], rhs=B["XT"][0:rows, h, 0:rows], start=True, stop=True)
                            ins.then_inc(s_xp, 1)
                    pe.wait_ge(s_xx, 4 * (L0 + levels(t)))
                    pe.wait_ge(s_vec, 7 * (u + 1))
                    pe.wait_ge(s_at, 4 * (u + 1))
                    for h in range(NH):
                        nc.tensor.matmul(bank[5][0:rows, h * HD:(h + 1) * HD], lhsT=B["XT"][0:rows, h, 0:rows], rhs=B["vb"][0:rows, h, :], start=True, stop=True)
                    for h in range(NH):
                        ins = nc.tensor.matmul(bank[6][:, h * rows:(h + 1) * rows], lhsT=B["kbg"][0:rows, h, :], rhs=B["XT"][0:rows, h, 0:rows], start=True, stop=True)
                    ins.then_inc(s_uw, 1)
                    pe.wait_ge(s_uwc, 2 * (u + 1))
                    if t == PT:
                        for h in range(NH):
                            pe.wait_ge(s_sS, 16 * NH)
                            for half in range(2):
                                if h:
                                    pe.wait_ge(s_sTc, 2 * (h - 1) + half + 1)
                                for b in range(4):
                                    ins = nc.tensor.transpose(bank[2 + half][:, b * HD:(b + 1) * HD], B["sS"][:, h, 4 * half + b, :], c("ident"))
                                ins.then_inc(s_sT, 1)
                            pe.wait_ge(s_sTc, 2 * (h + 1))
                            for b in range(DB):
                                ps = bank[4][:, :].rearrange("p (a h r) -> p a h r", a=2, h=NH)[:, :, h, b * DS:(b + 1) * DS]
                                ins = nc.tensor.matmul(ps, lhsT=B["sST"][:, b, :], rhs=B["wq"][:, :, h, b * DS:(b + 1) * DS], start=True, stop=True)
                            ins.then_inc(s_oT, 1)
                        pe.wait_ge(s_oTc, 1)
                        for h in range(NH):
                            ins = nc.tensor.matmul(bank[7][0:NSAMP, h * HD:(h + 1) * HD], lhsT=B["oT"][:, 0, h, :], rhs=c("ident"), start=True, stop=True)
                        ins.then_inc(s_pa, 1)
                        pe.wait_ge(s_dl, 1)
                        pe.wait_ge(s_eg, 3)
                        for h in range(NH):
                            ps = bank[0][0:NSAMP, h * HD:(h + 1) * HD]
                            nc.tensor.matmul(ps, lhsT=B["oT"][:, 1, h, :], rhs=c("ident"), start=True, stop=False)
                            ins = nc.tensor.matmul(ps, lhsT=B["PT"][0:NSAMP, h, 0:NSAMP], rhs=B["dl"][0:NSAMP, h, :], start=False, stop=True)
                        ins.then_inc(s_po, 1)
                        for h in range(NH):
                            pe.wait_ge(s_kdw, h + 1)
                            if h:
                                pe.wait_ge(s_snd, 3 * h)
                            for half in range(2):
                                ins = nc.tensor.matmul(bank[5 + half][:, :], lhsT=B["dl"][0:NSAMP, h, :], rhs=B["kdw"][:, 4 * half:4 * half + 4, :].rearrange("p b k -> p (b k)"), start=True, stop=True)
                            ins.then_inc(s_sn, 1)
                    pe.wait_ge(s_st0, 1)
                    for r0, n, _ in chunks(t):
                        ST = B["ST"][:, n_chunk % 2]
                        if n_chunk:
                            pe.wait_ge(s_st, NH * n_chunk)
                        for h in range(NH):
                            ins = nc.tensor.matmul(bank[7][r0:r0 + n, h * HD:(h + 1) * HD], lhsT=B["wq"][:, 0, h, r0:r0 + n], rhs=ST[:, h, :], start=True, stop=True)
                        ins.then_inc(s_pa, 1)
                        pe.wait_ge(s_dl, n_chunk + 2)
                        pe.wait_ge(s_dT, NH * (u + 1))
                        for h in range(NH):
                            ins = nc.tensor.matmul(bank[1][:, h * HD:(h + 1) * HD], lhsT=B["kd"][r0:r0 + n, h, :], rhs=B["dl"][r0:r0 + n, h, :], start=True, stop=True)
                        ins.then_inc(s_pst, 1)
                        pe.wait_ge(s_eg, 3 * (u + 1))
                        for h in range(NH):
                            ps = bank[0][r0:r0 + n, h * HD:(h + 1) * HD]
                            nc.tensor.matmul(ps, lhsT=B["wq"][:, 1, h, r0:r0 + n], rhs=ST[:, h, :], start=True, stop=False)
                            ins = nc.tensor.matmul(ps, lhsT=B["PT"][r0:r0 + n, h, r0:r0 + n], rhs=B["dl"][r0:r0 + n, h, :], start=False, stop=True)
                        ins.then_inc(s_po, 1)
                        n_chunk += 1
                pe.wait_ge(s_st, NH * n_chunk)
                for h in range(NH):
                    ins = nc.tensor.transpose(bank[2][:, h * HD:(h + 1) * HD], B["ST"][:, n_chunk % 2, h, :], c("ident"))
                ins.then_inc(s_fT, 1)
                for s_last, total in left_B:
                    pe.wait_ge(s_last, total)
                pe.wait_ge(s_vmeta, 16)

                def att_scores(u):
                    t, h = ATT[u]
                    r0, n, q0, nk = query_rows(t)
                    if u >= 2:
                        pe.wait_ge(s_sadd, 4 * (u - 1))
                        pe.wait_ge(s_wtc, 2 * (u - 1))
                    q = [qT[64 * a:64 * a + 64, h, q0:q0 + n] for a in range(2)]
                    k = [kT[64 * a:64 * a + 64, h, :] for a in range(2)]
                    meta = bank[4 + u % 2][r0:r0 + n, 0:2 * META]
                    nc.tensor.matmul(meta[:, 0:META], lhsT=q[0], rhs=k[0][:, 0:META], start=True, stop=True).then_inc(s_scm, 1)
                    for a in range(2):
                        nc.tensor.matmul(bank[2 * (u % 2) + a][r0:r0 + n, 0:nk], lhsT=q[a], rhs=k[a][:, META:META + nk], start=True, stop=True)
                    pe.wait_ge(s_scm, u + 1)
                    ins = nc.tensor.matmul(meta[:, META:], lhsT=q[1], rhs=k[1][:, 0:META], start=True, stop=True)
                    ins.then_inc(s_sc, 1)

                def att_values(u):
                    t, h = ATT[u]
                    r0, n, _, nk = query_rows(t)
                    w = C["S"][r0:r0 + n, u % 2, 0]
                    pe.wait_ge(s_wn, 4 * (u + 1))
                    if u:
                        pe.wait_ge(s_wtc, 2 * u)
                    for k in range(nk // 128):
                        nc.tensor.transpose(bank[6][:, k * 128:(k + 1) * 128], w[:, META + 128 * k:META + 128 * k + 128], c("ident"))
                    nc.tensor.transpose(bank[4 + u % 2][0:META, 128:128 + n], w[:, 0:META], c("ident", n, p0=r0)[:, r0:r0 + n]).then_inc(s_wt, 1)
                    pe.wait_ge(s_wtc, 2 * (u + 1))
                    if h == 0 and t:
                        pe.wait_ge(s_oa, 2 * t)
                    out = bank[7][r0:r0 + n, h * HD:(h + 1) * HD]
                    for k in range(nk // 128):
                        nc.tensor.matmul(out, lhsT=C["wT"][:, u % 2, 128 * k:128 * k + 128], rhs=vtok[:, k, h * HD:(h + 1) * HD], start=k == 0, stop=False)
                    nc.tensor.matmul(out, lhsT=C["wTm"][:, u % 2, 0:n], rhs=vmeta[:, h * HD:(h + 1) * HD], start=False, stop=True).then_inc(s_pv, 1)

                for u in range(len(ATT) + 1):
                    if u < len(ATT):
                        att_scores(u)
                    if u:
                        att_values(u - 1)

                def page_copied(n):
                    pe.wait_ge(s_kta if n % 2 == 0 else s_ktd, n // 2 + 1)

                def sample_values(p):
                    pe.wait_ge(s_dn, 3 * (p + 1))
                    if p:
                        pe.wait_ge(s_dwc, 2 * p)
                    for g in range(NPG):
                        nc.tensor.matmul(bank[5][:, 64 * g:64 * g + 64], lhsT=C["Sd"][:, p % 2, g * PAGE:(g + 1) * PAGE], rhs=C["fold"][:, :], start=True, stop=True)
                    nc.tensor.matmul(bank[6][0:NSAMP, 0:64], lhsT=C["Sd"][:, p % 2, PAST:], rhs=C["fold"][:, :], start=True, stop=True).then_inc(s_dw, 1)
                    pe.wait_ge(s_dwc, 2 * (p + 1))
                    for b in (2 * p, 2 * p + 1):
                        pe.wait_ge(s_vp[b % 3], 16 * NPG * (b // 3 + 1))
                        for h in range(NH):
                            out = bank[6][:, 128 + h * NSAMP + b * DS:128 + h * NSAMP + (b + 1) * DS]
                            wcol = 32 * (b % 2) + 8 * h
                            for g in range(NPG):
                                nc.tensor.matmul(out, lhsT=C["V"][:, b % 3, g, h * HD:(h + 1) * HD], rhs=C["wd"][:, g, wcol:wcol + DS], start=g == 0, stop=False)
                            ins = nc.tensor.matmul(out, lhsT=vtok[0:NSAMP, PT, h * HD:(h + 1) * HD], rhs=C["wd"][0:NSAMP, NPG, wcol:wcol + DS], start=False, stop=True)
                        ins.then_inc(s_dpv, 1)

                pe.wait_ge(s_qd, 2 * NH)
                for p in range(NPAIR):
                    for b in (2 * p, 2 * p + 1):
                        for g in range(NPG):
                            n = b * NPG + g
                            pe.wait_ge(s_kp[n % KRING], 16 * (n // KRING + 1))
                            if n >= 2:
                                page_copied(n - 2)
                            for h in range(NH):
                                ins = nc.tensor.transpose(bank[n % 2][:, h * PAGE:(h + 1) * PAGE], C["kpage"][:, n % KRING, h * HD:(h + 1) * HD], c("ident"))
                            ins.then_inc(s_ktp, 1)
                        page_copied(b * NPG + NPG - 2)
                        page_copied(b * NPG + NPG - 1)
                        if b % 2 == 0 and p:
                            pe.wait_ge(s_dadd, 4 * p)
                        r0 = 64 * (b % 2)
                        for half in range(2):
                            for h in range(NH):
                                nc.tensor.matmul(bank[2 + half][r0:r0 + 64, :], lhsT=C["Qd"][:, h, b, :], rhs=C["KT"][:, b % 2, h, 512 * half:512 * half + 512], start=h == 0, stop=h == NH - 1)
                        for h in range(NH):
                            ins = nc.tensor.matmul(bank[4][r0:r0 + 64, 0:NSAMP], lhsT=C["Qd"][:, h, b, :], rhs=kT[:, h, NPOS:TOK], start=h == 0, stop=h == NH - 1)
                        ins.then_inc(s_ds, 1)
                    if p:
                        sample_values(p - 1)
                sample_values(NPAIR - 1)
                pe.wait_ge(s_doc, 1)
                pe.wait_ge(s_oa, 2 * PT)
                for h in range(NH):
                    ins = nc.tensor.transpose(bank[7][0:NSAMP, h * HD:(h + 1) * HD], C["oTs"][:, h, :], c("ident"))
                ins.then_inc(s_dot, 1)

        nc.clear_and_free_semaphores(sems)
        nc.all_engine_barrier()
        sems.clear()
        front.close()

        def peer_buffer(name, shape, dt=F32):
            return ctx.enter_context(nc.sbuf_tensor("sb_" + name, shape, dt))

        hres = mix
        xn2 = peer_buffer("xn2", [128, NT, D])
        score = peer_buffer("score", [128, NT, SETS, NK])
        eidx = peer_buffer("eidx", [128, 2, SLOTS], U32)
        best = peer_buffer("best", [128, 2, HP, TOPK])
        gate = peer_buffer("gate", [128, 2, HP, TOPK])
        K = {name: peer_buffer(name, shape, dt) for name, (shape, dt) in {
            "hs": ([128, 2, NK], F32), "top": ([128, 2, TOPK], F32), "tix": ([128, 2, TOPK], U32), "tixf": ([128, 2, TOPK], F32),
            "cand": ([128, TOPK * TOPK], F32), "ctop": ([128, TOPK], F32), "cix": ([128, TOPK], U32), "cab": ([128, 2, TOPK], U32),
            "cabf": ([128, 2, TOPK], F32), "oh": ([128, 2, TOPK, TOPK], F32), "sel": ([128, 2, TOPK], F32), "e16": ([128, TOPK], U32),
        }.items()}
        P = stage({
            "wo": ([128, KC, D], F32), "mixT": ([128, KC, 128], F32), "x2": ([128, D], F32), "sq2": ([128, D], F32), "gain2": ([128, D], F32),
        } | {n: ([128, NT], F32) for n in ("ss2", "ms2", "rstd2")})
        with ExitStack() as over:
            over.enter_context(nc.sbuf_tensor("sb_skip", [128, 12 * D + 64], F32))
            xn2T = over.enter_context(nc.sbuf_tensor("sb_xn2T", [128, KC, OUT_TOK], F32))
            keysT = over.enter_context(nc.sbuf_tensor("sb_keysT", [128, SETS, NK], F32))
        Q = stage({"pwq": ([128, 2, KC, HW], F32), "q2T": ([128, 2, OUT_TOK], F32), "keys": ([128, 8, 128], F32)})
        s_tk = sem("topk_steps")
        s_idx = sem("experts_chosen")
        s_e16 = sem("expert_numbers")
        s_found = sem("dve_waits_passed")
        TK = 19
        s_wo = sem("w_out_loaded")
        s_g2 = sem("gain2_loaded")
        s_x2 = sem("x_loaded_again")
        s_keys = [sem(f"peer_keys_loaded{r}") for r in range(2)]
        s_kyp = sem("peer_keys_transposed")
        s_kyc = sem("peer_keys_copied")
        s_mxp = sem("mix_transposed")
        s_mxc = sem("mixT_copied")
        s_yp = sem("mixer_projected")
        s_h2 = sem("residual_added")
        s_ss2 = sem("residual_squares_summed")
        s_ms2 = sem("residual_mean_square")
        s_rs2 = sem("residual_rstd")
        s_xn2 = sem("residual_normed")
        s_x2p = sem("residual_transposed")
        s_x2c = sem("residualT_copied")
        s_wq = [sem(f"peer_wq_loaded{r}") for r in range(2)]
        s_q2p = sem("peer_queries")
        s_q2c = sem("peer_queries_copied")
        s_s2p = sem("peer_scores")
        s_s2c = sem("peer_scores_copied")

        GROUP = 8
        NGRP = SLOTS // GROUP
        E = stage({
            "us": ([128, GROUP, D], F32), "vs": ([128, GROUP, D], F32), "diag": ([128, 2, GROUP, 128], F32), "yt": ([128, D], F32),
            "gmax": ([128, HP, TOPK], F32), "gsum": ([128, HP], F32),
            "idc": ([128, 2, GROUP], U32), "h8": ([128, 2, GROUP], F32), "gel": ([128, 2, GROUP], F32), "w8": ([128, 2, GROUP], F32),
        })
        s_gt = sem("gate_exp")
        s_gtd = sem("gate_steps")
        s_passed = sem("pool_waits_passed")
        s_pe_passed = sem("pe_waits_passed")
        s_idc = sem("indices_copied")
        s_u = [sem(f"u_row{j}") for j in range(GROUP)]
        s_v = [sem(f"v_row{j}") for j in range(GROUP)]
        s_h = sem("activations")
        s_gel = sem("gelu")
        s_w8 = sem("expert_weights")
        s_dg = sem("weights_on_diagonal")
        s_y = sem("experts_summed")
        s_yo = sem("output_added")
        s_yst = sem("output_stored")
        YG = NGRP + 2

        stores = [(s_yst, 16 * NT)]

        with nc.Block() as block:

            @block.sync
            def _(sp):
                count = Count(sp)
                sp.dma_start(P["wo"][:, :, :], i["w_out"][0].rearrange("(k p) n -> p k n", p=128)).then_inc(s_wo, 16)
                for t in range(NT):
                    if t:
                        sp.wait_ge(s_h2, 2 * t)
                    if t < PT:
                        sp.dma_start(P["x2"][:, :], i["x_prompt"][0, 128 * t:128 * t + 128, :]).then_inc(s_x2, 16)
                    else:
                        sp.dma_start(P["x2"][0:NSAMP, :], i["x_sample"].rearrange("b s d -> (b s) d")).then_inc(s_x2, 16)
                sp.wait_ge(s_yp, NT)
                sp.wait_ge(s_h2, 2 * NT)
                sp.wait_ge(s_ss2, NT)
                sp.wait_ge(s_xn2, NT)
                keys = i["peer_keys"][0].rearrange("h c n d -> n (h c) d")
                wq = i["peer_wq"][0].rearrange("(k p) n -> p k n", p=128)
                for half in range(2):
                    if half:
                        sp.wait_ge(s_kyp, 2)
                    sp.dma_start(Q["keys"][:, :, :], keys[:, 8 * half:8 * half + 8, :]).then_inc(s_keys[half], 16)
                for g in range(4):
                    if g >= 2:
                        sp.wait_ge(s_q2p, 4 * (g - 1))
                    sp.dma_start(Q["pwq"][:, g % 2, :, :], wq[:, :, HW * g:HW * (g + 1)]).then_inc(s_wq[g % 2], 16)
                for t in range(NT):
                    sp.wait_ge(s_yo, 2 * (t + 1))
                    if t < PT:
                        sp.dma_start(o["y_prompt"][0, 128 * t:128 * t + 128, :], E["yt"][:, :]).then_inc(s_yst, 16)
                    else:
                        sp.dma_start(o["y_sample"].rearrange("b s d -> (b s) d"), E["yt"][0:NSAMP, :]).then_inc(s_yst, 16)
                for s_out, total in stores:
                    sp.wait_ge(s_out, total)

            @block.gpsimd
            def _(pool):
                count = Count(pool)
                pool.dma_start(P["gain2"][:, :], i["norm2"][0:1, :].broadcast_to([128, D])).then_inc(s_g2, 16)
                for t in range(NT):
                    rows = OUT_ROWS[t]
                    pool.wait_ge(s_ms2, t + 1)
                    nc.gpsimd.tensor_tensor(P["rstd2"][0:rows, t:t + 1], P["ms2"][0:rows, t:t + 1], minus_half[0:rows, 0:1], ALU.pow).then_inc(s_rs2, 1)
                pool.wait_ge(s_q2p, SETS)
                pool.wait_ge(s_s2p, SETS)
                for t in range(NT):
                    rows = OUT_ROWS[t]
                    pool.wait_ge(s_idx, HP * (t + 1))
                    with pool.Fori(0, NGRP // 2) as ii:
                        for par in range(2):
                            n = NGRP * t + par
                            pool.wait_ge(s_y, 2 * ii + (YG * t + par + 1))
                            nc.gpsimd.tensor_copy(E["idc"][0:rows, par, :], eidx[0:rows, t % 2, bass.ds(ii * (2 * GROUP) + par * GROUP, GROUP)]).then_inc(s_idc, 1)
                            pool.wait_ge(s_h, 2 * GROUP * ii + (GROUP * n + 1))
                            pool.wait_ge(s_idc, 2 * ii + (n + 1))
                            pool.sem_inc(s_passed, 1)
                            for j in range(GROUP):
                                nc.gpsimd.indirect_dma_start(E["us"][0:rows, j, :], None, i["peer_u"][0], bass.IndirectOffsetOnAxis(ap=E["idc"][0:rows, par, j:j + 1], axis=0)).then_inc(s_u[j], 16)
                            pool.wait_ge(s_y, 2 * ii + (YG * t + par + 2))
                            pool.sem_inc(s_passed, 1)
                            for j in range(GROUP):
                                nc.gpsimd.indirect_dma_start(E["vs"][0:rows, j, :], None, i["peer_v"][0], bass.IndirectOffsetOnAxis(ap=E["idc"][0:rows, par, j:j + 1], axis=0)).then_inc(s_v[j], 16)

            @block.scalar
            def _(act):
                count = Count(act)
                for t in range(NT):
                    rows = OUT_ROWS[t]
                    for half in range(2):
                        act.wait_ge(s_mxp, 2 * t + half + 1)
                        if t:
                            act.wait_ge(s_yp, t)
                        nc.scalar.activation(P["mixT"][:, 4 * half:4 * half + 4, 0:rows], bank[half][:, 0:4 * rows].rearrange("p (k r) -> p k r", k=4), ACT.Copy).then_inc(s_mxc, 1)
                    act.wait_ge(s_h2, 2 * (t + 1))
                    if t:
                        act.wait_ge(s_ss2, t)
                    nc.scalar.activation(P["sq2"][0:rows, :], hres[0:rows, t, :], ACT.Square, accum_out=P["ss2"][0:rows, t:t + 1]).then_inc(s_ss2, 1)
                    for half in range(2):
                        act.wait_ge(s_x2p, 2 * t + half + 1)
                        nc.scalar.activation(xn2T[:, 4 * half:4 * half + 4, 128 * t:128 * t + rows], bank[4 + half][:, 0:4 * rows].rearrange("p (k r) -> p k r", k=4), ACT.Copy).then_inc(s_x2c, 1)
                for q in range(4):
                    act.wait_ge(s_kyp, q + 1)
                    nc.scalar.activation(keysT[:, 4 * q:4 * q + 4, :].rearrange("p s n -> p (s n)"), bank[6 + q % 2][:, :], ACT.Copy).then_inc(s_kyc, 1)
                for s in range(SETS):
                    act.wait_ge(s_q2p, s + 1)
                    if s >= 2:
                        act.wait_ge(s_s2p, s - 1)
                    nc.scalar.activation(Q["q2T"][:, s % 2, 0:SEQ], bank[s % 2][:, :], ACT.Copy).then_inc(s_q2c, 1)
                    nc.scalar.activation(Q["q2T"][:, s % 2, SEQ:OUT_TOK], bank[2 + s % 2][:, 0:NSAMP], ACT.Copy).then_inc(s_q2c, 1)
                def gate_exp(t):
                    rows = OUT_ROWS[t]
                    act.wait_ge(s_gtd, 4 * t + 1)
                    nc.scalar.activation(E["gmax"][0:rows, :, :], E["gmax"][0:rows, :, :], ACT.Exp).then_inc(s_gt, 1)

                gate_exp(0)
                for t in range(NT):
                    rows = OUT_ROWS[t]
                    with act.Fori(0, NGRP // 2) as ii:
                        for par in range(2):
                            n = NGRP * t + par
                            act.wait_ge(s_h, 2 * GROUP * ii + (GROUP * (n + 1) + 1))
                            nc.scalar.activation(E["gel"][0:rows, par, :], E["h8"][0:rows, par, :], ACT.Gelu).then_inc(s_gel, 1)
                            act.wait_ge(s_w8, 2 * ii + (n + 1))
                            act.wait_ge(s_y, 2 * ii + (YG * t + par + 1))
                            for j in range(GROUP):
                                nc.scalar.activation(E["diag"][0:rows, par, j, 0:rows], c("ident", rows, rows), ACT.Copy, scale=E["w8"][0:rows, par, j:j + 1]).then_inc(s_dg, 1)
                    if t + 1 < NT:
                        gate_exp(t + 1)

            @block.vector
            def _(dve):
                count = Count(dve)
                def choose(t, h):
                    rows = OUT_ROWS[t]
                    at = HP * t * TK + TK * h
                    R = {n: K[n][0:rows] for n in ("hs", "top", "tix", "tixf", "cand", "ctop", "cix", "cab", "cabf", "oh", "sel", "e16")}
                    steps = [0]

                    def step(ins, wait=False):
                        ins.then_inc(s_tk, 1)
                        steps[0] += 1
                        if wait:
                            dve.wait_ge(s_tk, at + steps[0])
                            dve.sem_inc(s_found, 1)

                    step(nc.vector.tensor_copy(R["hs"].rearrange("p a n -> p (a n)"), score[0:rows, t].rearrange("p s n -> p (s n)")[:, bass.ds(2 * NK * h, 2 * NK)]), True)
                    for k in range(0, TOPK, 8):
                        for a in range(2):
                            step(nc.vector.max(R["top"][:, a, k:k + 8], R["hs"][:, a]), a == 1)
                        for a in range(2):
                            nc.vector.max_index(R["tix"][:, a, k:k + 8], R["top"][:, a, k:k + 8], R["hs"][:, a])
                        if k == 0:
                            for a in range(2):
                                step(nc.vector.match_replace(R["hs"][:, a], R["top"][:, a, 0:8], R["hs"][:, a], NEG), a == 1)
                    step(nc.vector.tensor_tensor(R["cand"].rearrange("p (a b) -> p a b", a=TOPK), R["top"][:, 0].unsqueeze(2).broadcast_to([rows, TOPK, TOPK]),
                                                 R["top"][:, 1].unsqueeze(1).broadcast_to([rows, TOPK, TOPK]), ALU.add), True)
                    for k in range(0, TOPK, 8):
                        step(nc.vector.max(R["ctop"][:, k:k + 8], R["cand"]), True)
                        nc.vector.max_index(R["cix"][:, k:k + 8], R["ctop"][:, k:k + 8], R["cand"])
                        if k == 0:
                            step(nc.vector.match_replace(R["cand"], R["ctop"][:, 0:8], R["cand"], NEG), True)
                    step(nc.vector.tensor_copy(R["tixf"], R["tix"]), True)
                    step(nc.vector.tensor_scalar(R["cab"][:, 0], R["cix"], 4, None, ALU.logical_shift_right))
                    step(nc.vector.tensor_scalar(R["cab"][:, 1], R["cix"], TOPK - 1, None, ALU.bitwise_and), True)
                    step(nc.vector.tensor_copy(R["cabf"], R["cab"]), True)
                    iota = c("iota", rows).unsqueeze(1).broadcast_to([rows, TOPK, TOPK])
                    for a in range(2):
                        nc.vector.tensor_tensor(R["oh"][:, a], iota, R["cabf"][:, a].unsqueeze(2).broadcast_to([rows, TOPK, TOPK]), ALU.is_equal)
                    step(nc.vector.tensor_copy(best[0:rows, t % 2].rearrange("p h k -> p (h k)")[:, bass.ds(TOPK * h, TOPK)], R["ctop"]), True)
                    for a in range(2):
                        step(nc.vector.tensor_tensor(R["oh"][:, a], R["oh"][:, a], R["tixf"][:, a].unsqueeze(1).broadcast_to([rows, TOPK, TOPK]), ALU.mult), a == 1)
                    step(nc.vector.tensor_reduce(R["sel"], R["oh"], AX.X, ALU.add), True)
                    assert steps[0] == TK, steps
                    nc.vector.scalar_tensor_tensor(R["e16"], R["sel"][:, 0], float(NK), R["sel"][:, 1], ALU.mult, ALU.add).then_inc(s_e16, 1)
                    dve.wait_ge(s_e16, HP * t + 1 + h)
                    nc.vector.tensor_copy(eidx[0:rows, t % 2, bass.ds(TOPK * h, TOPK)], R["e16"]).then_inc(s_idx, 1)

                dve.wait_ge(s_g2, 16)
                for t in range(NT):
                    rows = OUT_ROWS[t]
                    dve.wait_ge(s_yp, t + 1)
                    dve.wait_ge(s_x2, 16 * (t + 1))
                    for half in range(2):
                        cols = slice(512 * half, 512 * half + 512)
                        nc.vector.tensor_tensor(hres[0:rows, t, cols], bank[2 + half][0:rows, :], P["x2"][0:rows, cols], ALU.add).then_inc(s_h2, 1)
                    dve.wait_ge(s_ss2, t + 1)
                    nc.vector.tensor_scalar(P["ms2"][0:rows, t:t + 1], P["ss2"][0:rows, t:t + 1], 1.0 / D, EPS, ALU.mult, ALU.add).then_inc(s_ms2, 1)
                    dve.wait_ge(s_rs2, t + 1)
                    nc.vector.scalar_tensor_tensor(xn2[0:rows, t, :], hres[0:rows, t, :], P["rstd2"][0:rows, t:t + 1], P["gain2"][0:rows, :], ALU.mult, ALU.mult).then_inc(s_xn2, 1)
                for s in range(SETS):
                    dve.wait_ge(s_s2p, s + 1)
                    nc.vector.tensor_copy(score[:, 0:PT, s, :], bank[4 + s % 2][:, :].rearrange("p (t n) -> p t n", t=PT)).then_inc(s_s2c, 1)
                    nc.vector.tensor_copy(score[0:NSAMP, PT, s, :], bank[6 + s % 2][0:NSAMP, 0:NK]).then_inc(s_s2c, 1)
                    if s % 2:
                        dve.wait_ge(s_s2c, 2 * (s + 1))
                        choose(0, s // 2)
                dve.wait_ge(s_q2p, SETS)
                dve.wait_ge(s_s2p, SETS)
                dve.wait_ge(s_s2c, 2 * SETS)

                def gates_start(t):
                    rows = OUT_ROWS[t]
                    dve.wait_ge(s_idx, HP * (t + 1))
                    b = best[0:rows, t % 2]
                    count.inc(nc.vector.tensor_tensor(E["gmax"][0:rows], b, b[:, :, 0:1].broadcast_to([rows, HP, TOPK]), ALU.subtract), s_gtd)

                def gates_end(t):
                    rows = OUT_ROWS[t]
                    m = E["gmax"][0:rows]
                    dve.wait_ge(s_gt, t + 1)
                    count.done(nc.vector.tensor_reduce(E["gsum"][0:rows, :], m, AX.X, ALU.add), s_gtd)
                    count.done(nc.vector.reciprocal(E["gsum"][0:rows, :], E["gsum"][0:rows, :]), s_gtd)
                    count.done(nc.vector.tensor_tensor(gate[0:rows, t % 2], m, E["gsum"][0:rows, :].unsqueeze(2).broadcast_to([rows, HP, TOPK]), ALU.mult), s_gtd)

                def products(t, ii, par):
                    rows, n = OUT_ROWS[t], NGRP * t + par
                    for j in range(GROUP):
                        dve.wait_ge(s_u[j], 32 * ii + 16 * (n + 1))
                        nc.vector.tensor_tensor_reduce(out=E["us"][0:rows, j, :], in0=E["us"][0:rows, j, :], in1=xn2[0:rows, t, :], scale=1.0, scalar=0.0,
                                                       op0=ALU.mult, op1=ALU.add, accum_out=E["h8"][0:rows, par, j:j + 1]).then_inc(s_h, 1)

                def weights(t, ii, par):
                    rows, n = OUT_ROWS[t], NGRP * t + par
                    dve.wait_ge(s_gel, 2 * ii + (n + 1))
                    g8 = gate[0:rows, t % 2].rearrange("p h k -> p (h k)")[:, bass.ds(2 * GROUP * ii + GROUP * par, GROUP)]
                    nc.vector.tensor_tensor(E["w8"][0:rows, par, :], E["gel"][0:rows, par, :], g8, ALU.mult).then_inc(s_w8, 1)

                def output(t):
                    rows = OUT_ROWS[t]
                    dve.wait_ge(s_y, YG * (t + 1) + 1)
                    if t:
                        dve.wait_ge(s_yst, 16 * t)
                    for half in range(2):
                        cols = slice(512 * half, 512 * half + 512)
                        nc.vector.tensor_tensor(E["yt"][0:rows, cols], bank[2 * (t % 2) + half][0:rows, :], hres[0:rows, t, cols], ALU.add).then_inc(s_yo, 1)

                dve.sem_inc(s_h, 1)
                gates_start(0)
                for t in range(NT):
                    products(t, 0, 0)
                    gates_end(t)
                    weights(t, 0, 0)
                    products(t, 0, 1)
                    weights(t, 0, 1)
                    if t:
                        output(t - 1)
                    if t + 1 < NT:
                        choose(t + 1, 0)
                    with dve.Fori(1, NGRP // 2) as ii:
                        for par in range(2):
                            products(t, ii, par)
                            weights(t, ii, par)
                        if t + 1 < NT:
                            choose(t + 1, ii)
                    if t + 1 < NT:
                        gates_start(t + 1)
                output(NT - 1)

            @block.tensor
            def _(pe):
                count = Count(pe)
                for t in range(NT):
                    rows = OUT_ROWS[t]
                    for half in range(2):
                        if t:
                            pe.wait_ge(s_mxc, 2 * (t - 1) + half + 1)
                        for k in range(4):
                            kk = 4 * half + k
                            ins = nc.tensor.transpose(bank[half][:, k * rows:(k + 1) * rows], mix[0:rows, t, kk * 128:(kk + 1) * 128], c("ident", rows, rows))
                        ins.then_inc(s_mxp, 1)
                    if t == 0:
                        pe.wait_ge(s_wo, 16)
                    pe.wait_ge(s_mxc, 2 * (t + 1))
                    if t:
                        pe.wait_ge(s_h2, 2 * t)
                    for half in range(2):
                        for k in range(KC):
                            ins = nc.tensor.matmul(bank[2 + half][0:rows, :], lhsT=P["mixT"][:, k, 0:rows], rhs=P["wo"][:, k, 512 * half:512 * half + 512], start=k == 0, stop=k == KC - 1)
                    ins.then_inc(s_yp, 1)
                    pe.wait_ge(s_xn2, t + 1)
                    for half in range(2):
                        if t:
                            pe.wait_ge(s_x2c, 2 * (t - 1) + half + 1)
                        for k in range(4):
                            kk = 4 * half + k
                            ins = nc.tensor.transpose(bank[4 + half][:, k * rows:(k + 1) * rows], xn2[0:rows, t, kk * 128:(kk + 1) * 128], c("ident", rows, rows))
                        ins.then_inc(s_x2p, 1)
                for q in range(4):
                    pe.wait_ge(s_keys[q // 2], 16)
                    if q >= 2:
                        pe.wait_ge(s_kyc, q - 1)
                    for k in range(4):
                        ins = nc.tensor.transpose(bank[6 + q % 2][:, k * 128:(k + 1) * 128], Q["keys"][:, (4 * q + k) % 8, :], c("ident"))
                    ins.then_inc(s_kyp, 1)
                pe.wait_ge(s_mxc, 2 * NT)
                pe.wait_ge(s_h2, 2 * NT)
                pe.wait_ge(s_x2c, 2 * NT)
                pe.wait_ge(s_kyc, 4)

                def peer_scores(s):
                    pe.wait_ge(s_q2c, 2 * (s + 1))
                    if s >= 2:
                        pe.wait_ge(s_s2c, 2 * (s - 1))
                    for t in range(PT):
                        nc.tensor.matmul(bank[4 + s % 2][:, t * NK:(t + 1) * NK], lhsT=Q["q2T"][:, s % 2, 128 * t:128 * t + 128], rhs=keysT[:, s, :], start=True, stop=True)
                    nc.tensor.matmul(bank[6 + s % 2][0:NSAMP, 0:NK], lhsT=Q["q2T"][:, s % 2, SEQ:OUT_TOK], rhs=keysT[:, s, :], start=True, stop=True).then_inc(s_s2p, 1)

                for s in range(SETS):
                    g, col = s // 4, 128 * (s % 4)
                    if s % 4 == 0:
                        pe.wait_ge(s_wq[g % 2], 16 * (g // 2 + 1))
                    if s >= 2:
                        pe.wait_ge(s_q2c, 2 * (s - 1))
                    for k in range(KC):
                        nc.tensor.matmul(bank[s % 2][:, :], lhsT=Q["pwq"][:, g % 2, k, col:col + 128], rhs=xn2T[:, k, 0:SEQ], start=k == 0, stop=k == KC - 1)
                    for k in range(KC):
                        ins = nc.tensor.matmul(bank[2 + s % 2][:, 0:NSAMP], lhsT=Q["pwq"][:, g % 2, k, col:col + 128], rhs=xn2T[:, k, SEQ:OUT_TOK], start=k == 0, stop=k == KC - 1)
                    ins.then_inc(s_q2p, 1)
                    if s:
                        peer_scores(s - 1)
                peer_scores(SETS - 1)
                for s in range(SETS - 2, SETS):
                    pe.wait_ge(s_s2c, 2 * (s + 1))
                    pe.wait_ge(s_q2c, 2 * (s + 1))

                def zero(t, first):
                    for half in range(2):
                        ins = nc.tensor.matmul(bank[2 * (t % 2) + half][0:OUT_ROWS[t], :], lhsT=c("meta_rows", 1, OUT_ROWS[t]), rhs=c("bias_past", 1)[:, 0:512], start=first, stop=not first)
                    ins.then_inc(s_y, 1)

                pe.sem_inc(s_y, 1)
                for t in range(NT):
                    rows = OUT_ROWS[t]
                    if t >= 2:
                        pe.wait_ge(s_yo, 2 * (t - 1))
                    zero(t, True)
                    with pe.Fori(0, NGRP // 2) as ii:
                        for par in range(2):
                            n = NGRP * t + par
                            for j in range(GROUP):
                                pe.wait_ge(s_dg, 2 * GROUP * ii + (GROUP * n + j + 1))
                                pe.wait_ge(s_v[j], 32 * ii + 16 * (n + 1))
                                if rows < 128:
                                    pe.sem_inc(s_pe_passed, 1)
                                for half in range(2):
                                    ins = nc.tensor.matmul(bank[2 * (t % 2) + half][0:rows, :], lhsT=E["diag"][0:rows, par, j, 0:rows],
                                                           rhs=E["vs"][0:rows, j, 512 * half:512 * half + 512], start=False, stop=False)
                            ins.then_inc(s_y, 1)
                    zero(t, False)


INPUTS = ["x_prompt", "x_sample", "cache_k", "cache_v", "state_ssm", "state_conv", "page_table", "meta_tokens", "norm1", "w_in",
          "conv_w", "q_norm", "k_norm", "lam_q1", "lam_k1", "lam_q2", "lam_k2", "attn_subln", "a_log", "dt_bias", "gdn_norm",
          "w_out", "norm2", "peer_wq", "peer_keys", "peer_u", "peer_v"]
OUTPUTS = {"y_prompt": (1, SEQ, D), "y_sample": (DB, DS, D), "k_prompt": (1, 1, NPOS, NH, HD), "v_prompt": (1, 1, NPOS, NH, HD),
           "k_sample": (1, DB, DS, NH, HD), "v_sample": (1, DB, DS, NH, HD), "ssm_prompt": (1, 1, NH, HD, HD),
           "ssm_sample": (1, DB, NH, HD, HD), "conv_prompt": (1, 1, CONV_W - 1, CONV), "conv_sample": (1, DB, CONV_W - 1, CONV)}


def kernel(**inputs):
    import concourse.bacc as bacc
    from concourse.bass_utils import run_bass_kernel_spmd

    nc = bacc.Bacc("TRN2", target_bir_lowering=False, num_devices=1)
    arrays, i = {}, {}
    for name in INPUTS:
        a = np.ascontiguousarray(inputs[name])
        arrays["in_" + name] = a
        i[name] = nc.dram_tensor("in_" + name, a.shape, mybir.dt.from_np(a.dtype), kind="ExternalInput").ap()
    o = {name: nc.dram_tensor("out_" + name, shape, F32, kind="ExternalOutput").ap() for name, shape in OUTPUTS.items()}
    table = nc.inline_tensor(np.ascontiguousarray(np.concatenate(list(CONSTS.values()), axis=1)), "shape_tables").ap()
    hybrid_step(nc, i, o, table)
    r = run_bass_kernel_spmd(nc, [arrays], core_ids=[0])
    return tuple(r.results[0]["out_" + name] for name in OUTPUTS)
```
